# Optimizing a Trainium2 kernel written in Bass

```python
import jax, jax.numpy as jnp
from jax import lax
import numpy as np

D_MODEL = 1024
BATCH = 1
SEQ = 512
DEPTH = 2
DEC_BATCH = 1
DEC_SEQ = 64
PAST_LEN = 128

CHUNK = 64
N_A = DEPTH // 2
N_B = DEPTH - N_A
MLP_CHUNK = 128
GMLP_GROUPS = 8
D_GATE = D_MODEL
GMLP_GC = D_GATE // GMLP_GROUPS
N_HEADS = 16
N_KV_HEADS = 4
HEAD_DIM = D_MODEL // N_HEADS
GQA_GROUP = N_HEADS // N_KV_HEADS
WINDOW = 128
WIN_CHUNKS = WINDOW // CHUNK
PEER_HEADS = 8
N_KEYS = 128
N_EXPERTS = N_KEYS * N_KEYS
PEER_TOPK = 16
D_KEY = 256
D_HALF = D_KEY // 2
PEER_BLOCK = 512
EPS = 1e-6
NEG = -1e30

kernel_name = "yoco_gmlp_swa_sink_alibi_peer_stream_step"

def rms_norm(x, g):
    xf = x.astype(jnp.float32)
    y = xf * lax.rsqrt(jnp.mean(xf * xf, axis=-1, keepdims=True) + EPS)
    return (y * g.astype(jnp.float32)).astype(x.dtype)

def alibi_slopes(n):
    return jnp.array([2.0 ** (-8.0 * (h + 1) / n) for h in range(n)], dtype=jnp.float32)

def gmlp_mix(xn, w_in, g_v, w_s, b_s, w_out):
    B, L, _ = xn.shape
    hmid = jax.nn.gelu(xn @ w_in)
    u, v = jnp.split(hmid, 2, axis=-1)
    v = rms_norm(v, g_v)
    lc = min(L, MLP_CHUNK)
    nc = L // lc
    pos = jnp.arange(lc)
    mask = (pos[None, :] // CHUNK) <= (pos[:, None] // CHUNK)
    ws = jnp.where(mask[None], w_s[:, :lc, :lc], jnp.zeros((), w_s.dtype))
    vb = v.reshape(B, nc, lc, GMLP_GROUPS, GMLP_GC)
    mixed = jnp.einsum('gij,bnjgc->bnigc', ws, vb) + b_s[:, :lc].T[None, None, :, :, None]
    out = u * mixed.reshape(B, L, D_GATE)
    return out @ w_out, v

def banded_attention(q, k, v, q_pos, k_pos, k_valid, slopes, sink):
    B, NB, Lq = q.shape[:3]
    qg = q.reshape(B, NB, Lq, N_KV_HEADS, GQA_GROUP, HEAD_DIM)
    s = jnp.einsum('bnqkgd,bnskd->bnkgqs', qg, k).astype(jnp.float32) * (HEAD_DIM ** -0.5)
    dist = jnp.abs(q_pos[:, :, None] - k_pos[:, None, :]).astype(jnp.float32)
    s = s - slopes.reshape(N_KV_HEADS, GQA_GROUP)[None, None, :, :, None, None] * dist[None, :, None, None]
    s = jnp.where(k_valid[None, :, None, None, None, :], s, NEG)
    sink_col = jnp.broadcast_to(
        sink.astype(jnp.float32).reshape(N_KV_HEADS, GQA_GROUP)[None, None, :, :, None, None],
        s.shape[:-1] + (1,))
    p = jax.nn.softmax(jnp.concatenate([s, sink_col], axis=-1), axis=-1)[..., :-1]
    o = jnp.einsum('bnkgqs,bnskd->bnqkgd', p.astype(v.dtype), v)
    return o.reshape(B, NB, Lq, N_HEADS * HEAD_DIM)

def prompt_window_attention(q, k, v, slopes, sink):
    B, L = q.shape[:2]
    nb = L // CHUNK
    qb = q.reshape(B, nb, CHUNK, N_HEADS, HEAD_DIM)

    def band(t):
        tp = jnp.pad(t, ((0, 0), (WINDOW, 0), (0, 0), (0, 0)))
        tp = tp.reshape(B, nb + WIN_CHUNKS, CHUNK, N_KV_HEADS, HEAD_DIM)
        return jnp.concatenate([tp[:, i:i + nb] for i in range(WIN_CHUNKS + 1)], axis=2)

    c0 = jnp.arange(nb)[:, None] * CHUNK
    q_pos = c0 + jnp.arange(CHUNK)[None]
    k_pos = c0 - WINDOW + jnp.arange(WINDOW + CHUNK)[None]
    o = banded_attention(qb, band(k), band(v), q_pos, k_pos, k_pos >= 0, slopes, sink)
    return o.reshape(B, L, N_HEADS * HEAD_DIM)

def cached_window_attention(q, k_new, v_new, ck, cv, slopes, sink):
    B, L = q.shape[:2]
    wc = ck.shape[1]
    kc = jnp.concatenate([ck, k_new], axis=1)
    vc = jnp.concatenate([cv, v_new], axis=1)
    q_pos = (PAST_LEN + jnp.arange(L))[None]
    k_pos = (PAST_LEN - wc + jnp.arange(wc + L))[None]
    valid = jnp.ones(k_pos.shape, dtype=bool)
    o = banded_attention(q[:, None], kc[:, None], vc[:, None], q_pos, k_pos, valid, slopes, sink)
    return o.reshape(B, L, N_HEADS * HEAD_DIM)

def peer_ffn(xn, w_q, sub_keys, exp_u, exp_v):
    T = xn.shape[0]
    blk = min(PEER_BLOCK, T)
    nblk = -(-T // blk)
    xp = jnp.pad(xn, ((0, nblk * blk - T), (0, 0))).reshape(nblk, blk, D_MODEL)

    def one_block(xb):
        q = (xb @ w_q).reshape(blk, PEER_HEADS, 2, D_HALF)
        sc = jnp.einsum('thpd,hpnd->thpn', q, sub_keys).astype(jnp.float32)
        top_s, top_i = lax.top_k(sc, PEER_TOPK)
        cand_s = top_s[:, :, 0, :, None] + top_s[:, :, 1, None, :]
        cand_i = top_i[:, :, 0, :, None] * N_KEYS + top_i[:, :, 1, None, :]
        best_s, sel = lax.top_k(cand_s.reshape(blk, PEER_HEADS, PEER_TOPK * PEER_TOPK), PEER_TOPK)
        idx = jnp.take_along_axis(cand_i.reshape(blk, PEER_HEADS, PEER_TOPK * PEER_TOPK), sel, axis=-1)
        gate = jax.nn.softmax(best_s, axis=-1)
        act = jax.nn.gelu(jnp.einsum('thkd,td->thk', exp_u[idx], xb))
        w = (gate * act.astype(jnp.float32)).astype(xb.dtype)
        return jnp.einsum('thk,thkd->td', w, exp_v[idx])

    return lax.map(one_block, xp).reshape(nblk * blk, D_MODEL)[:T]

def setup_inputs(seed: int = 0) -> dict:
    key = jax.random.key(seed)
    ks = jax.random.split(key, 24)
    f32 = jnp.float32
    nrm = lambda k, shape, s: jax.random.normal(k, shape, f32) * s
    w_cache = min(WINDOW, PAST_LEN)
    return {
        'x_prompt': nrm(ks[0], (BATCH, SEQ, D_MODEL), 1.0),
        'x_sample': nrm(ks[1], (DEC_BATCH, DEC_SEQ, D_MODEL), 1.0),
        'cache_k_win': nrm(ks[2], (DEC_BATCH, w_cache, N_KV_HEADS, HEAD_DIM), 1.0),
        'cache_v_win': nrm(ks[3], (DEC_BATCH, w_cache, N_KV_HEADS, HEAD_DIM), 1.0),
        'norm_mix': 1.0 + nrm(ks[4], (DEPTH, D_MODEL), 0.05),
        'norm_ffn': 1.0 + nrm(ks[5], (DEPTH, D_MODEL), 0.05),
        'gmlp_w_in': nrm(ks[6], (N_A, D_MODEL, 2 * D_GATE), D_MODEL ** -0.5),
        'gmlp_norm_v': 1.0 + nrm(ks[7], (N_A, D_GATE), 0.05),
        'gmlp_w_s': nrm(ks[8], (N_A, GMLP_GROUPS, MLP_CHUNK, MLP_CHUNK), MLP_CHUNK ** -0.5),
        'gmlp_b_s': 1.0 + nrm(ks[9], (N_A, GMLP_GROUPS, MLP_CHUNK), 0.1),
        'gmlp_w_out': nrm(ks[10], (N_A, D_GATE, D_MODEL), D_GATE ** -0.5),
        'norm_kv': 1.0 + nrm(ks[11], (D_MODEL,), 0.05),
        'w_kv': nrm(ks[12], (D_MODEL, 2 * N_KV_HEADS * HEAD_DIM), D_MODEL ** -0.5),
        'attn_w_q': nrm(ks[13], (N_B, D_MODEL, N_HEADS * HEAD_DIM), D_MODEL ** -0.5),
        'attn_sinks': nrm(ks[14], (N_B, N_HEADS), 0.5),
        'attn_w_o': nrm(ks[15], (N_B, N_HEADS * HEAD_DIM, D_MODEL), (N_HEADS * HEAD_DIM) ** -0.5),
        'peer_w_q': nrm(ks[16], (DEPTH, D_MODEL, PEER_HEADS * D_KEY), D_MODEL ** -0.5),
        'peer_sub_keys': nrm(ks[17], (DEPTH, PEER_HEADS, 2, N_KEYS, D_HALF), D_HALF ** -0.5),
        'peer_u': nrm(ks[18], (DEPTH, N_EXPERTS, D_MODEL), D_MODEL ** -0.5),
        'peer_v': nrm(ks[19], (DEPTH, N_EXPERTS, D_MODEL), 0.25),
        'norm_final': 1.0 + nrm(ks[20], (D_MODEL,), 0.05),
    }

def reference(x_prompt, x_sample, cache_k_win, cache_v_win, norm_mix, norm_ffn,
              gmlp_w_in, gmlp_norm_v, gmlp_w_s, gmlp_b_s, gmlp_w_out, norm_kv, w_kv,
              attn_w_q, attn_sinks, attn_w_o, peer_w_q, peer_sub_keys, peer_u, peer_v,
              norm_final):
    slopes = alibi_slopes(N_HEADS)

    def trunk(x, ck, cv):
        prompt = ck is None
        B, L, _ = x.shape
        h = x
        k_sh = None
        v_sh = None
        gmlp_rows = []
        for l in range(DEPTH):
            hn = rms_norm(h, norm_mix[l])
            if l < N_A:
                y, v_rows = gmlp_mix(hn, gmlp_w_in[l], gmlp_norm_v[l], gmlp_w_s[l],
                                     gmlp_b_s[l], gmlp_w_out[l])
                gmlp_rows.append(v_rows)
            else:
                j = l - N_A
                q = (hn @ attn_w_q[j]).reshape(B, L, N_HEADS, HEAD_DIM)
                if prompt:
                    o = prompt_window_attention(q, k_sh, v_sh, slopes, attn_sinks[j])
                else:
                    o = cached_window_attention(q, k_sh, v_sh, ck, cv, slopes, attn_sinks[j])
                y = o @ attn_w_o[j]
            h = h + y
            hf = rms_norm(h, norm_ffn[l]).reshape(B * L, D_MODEL)
            h = h + peer_ffn(hf, peer_w_q[l], peer_sub_keys[l], peer_u[l], peer_v[l]).reshape(B, L, D_MODEL)
            if l == N_A - 1:
                kv = (rms_norm(h, norm_kv) @ w_kv).reshape(B, L, 2, N_KV_HEADS, HEAD_DIM)
                k_sh = kv[:, :, 0]
                v_sh = kv[:, :, 1]
        return rms_norm(h, norm_final), k_sh, v_sh, gmlp_rows

    y_prompt, k_p, v_p, _ = trunk(x_prompt, None, None)
    prompt_k_win = k_p[:, -WINDOW:]
    prompt_v_win = v_p[:, -WINDOW:]

    y_sample, k_s, v_s, rows_s = trunk(x_sample, cache_k_win, cache_v_win)
    wc = cache_k_win.shape[1]
    sample_k_win = jnp.concatenate([cache_k_win, k_s], axis=1)[:, -wc:]
    sample_v_win = jnp.concatenate([cache_v_win, v_s], axis=1)[:, -wc:]
    sample_gmlp_v = jnp.stack(rows_s, axis=0)

    return (y_prompt, y_sample, prompt_k_win, prompt_v_win, sample_k_win, sample_v_win, sample_gmlp_v)


_drawn_inputs = setup_inputs


def setup_inputs(seed=0):
    import zlib

    import numpy as np

    out = dict(_drawn_inputs(seed))
    spreads = {}
    factors = {'attn_sinks': 3.252}
    for name, (base, spread) in spreads.items():
        noise = np.random.default_rng([zlib.crc32(name.encode()), seed]).standard_normal(out[name].shape)
        drawn = base * np.exp(spread * noise) if base else spread * noise
        out[name] = __import__('jax').numpy.asarray(drawn.astype(out[name].dtype))
    for name, factor in factors.items():
        out[name] = (out[name] * factor).astype(out[name].dtype)
    return out
```

```python
from contextlib import ExitStack

import numpy as np
import concourse.bass as bass
from concourse import mybir

F32, F32R, F16, U32 = mybir.dt.float32, mybir.dt.float32r, mybir.dt.float16, mybir.dt.uint32
ALU = mybir.AluOpType
ACT = mybir.ActivationFunctionType
AX = mybir.AxisListType.X

P = 128
D, SEQ, DEC = 1024, 512, 64
T = SEQ + DEC
TH = T // 2
DT = D // P
TCS = [128, 128, 128, 128, 64]
NTC = len(TCS)
GROUPS = 8
HEADS, KVH, DH = 16, 4, 64
PH, TOPK, NK = 8, 16, 128
HP = 2 * PH
EPS = 1e-6
CHUNK = 16
NPAIR = NK // 2
STEPS = CHUNK // 2
TB = 12
NB = T // STEPS // TB
GS = 4096.0
AHEAD = 16
MAIN = NPAIR - AHEAD
NEGBIG = -3.0e38
ROWS = [TOPK // (a + 1) for a in range(TOPK // 2)]
OFFS = [sum(ROWS[:a]) for a in range(TOPK // 2 + 1)]
NC = OFFS[-1] + TOPK // 2
LIN = {"in": 16, "out": 8, "pq0": 16, "kv": 4, "q": 8, "o": 8, "pq1": 16}
G_MIX0, G_V, G_FFN0, G_KV, G_MIX1, G_FFN1, G_FIN = range(7)


def plan():
    fills, pieces, tile = [1] * 8, 0, 0
    base, kb, t0 = {}, {}, {}

    def seg(name, **use):
        base[name] = list(fills)
        for b, n in use.items():
            fills[int(b[1:])] += n

    def lin(name):
        nonlocal pieces, tile
        n = LIN[name]
        kb[name], t0[name] = pieces, tile
        pieces += n // 4
        tile += n
        return {f"b{b}": n // 2 for b in range(4)}

    def peer(l):
        nonlocal pieces
        seg(f"pq{l}", **lin(f"pq{l}"))
        seg(f"sc{l}", b4=8, b5=8, b6=8, b7=8)
        seg(f"gt{l}", b4=3, b5=2)
        seg(f"bld{l}", b6=NPAIR * NB // 2, b7=NPAIR * NB // 2)
        kb[f"peer{l}"] = pieces
        pieces += NPAIR
        seg(f"peer{l}", b0=2 * NPAIR, b1=2 * NPAIR, b2=4 * NPAIR, b3=4 * NPAIR, b4=4 * NPAIR, b5=4 * NPAIR)

    seg("n0", b1=1, b3=1)
    seg("in", **lin("in"))
    seg("n1", b1=1, b3=1)
    seg("vtr", b4=5, b5=5)
    seg("mix", b4=4, b5=4, b6=4, b7=4)
    seg("out", **lin("out"))
    seg("n2", b1=1, b3=1)
    peer(0)
    seg("n3", b1=1, b3=1)
    seg("kv", **lin("kv"))
    seg("q", **lin("q"))
    seg("vn", b6=3, b7=2)
    seg("att", **{f"b{b}": 20 for b in range(8)})
    seg("o", **lin("o"))
    seg("n4", b1=1, b3=1)
    peer(1)
    seg("n5", b1=1, b3=1)
    return base, kb, t0


def program(nc, xT, ckT, cv, gains, lin, uv, skT, wsT, bs, sinks, dist, ident_c, iota_a, iota_n, iota_c,
            yT, kvT, kwin, vwin, gv, parked):
    BASE, KB, T0 = plan()
    with ExitStack() as ctx:
        def sb(name, shape, dt):
            return ctx.enter_context(nc.sbuf_tensor(name, shape, dt))

        def sem(name):
            return ctx.enter_context(nc.semaphore(name))

        h = sb("h", [P, DT, T], F32)
        xh = sb("xh", [P, DT, T], F32R)
        xl = sb("xl", [P, DT, T], F32R)
        W = sb("W", [P, 2 * CHUNK * T], F32)
        raw = sb("raw", [P, 4, D], F32)
        wh = sb("wh", [P, 4, D], F32R)
        wl = sb("wl", [P, 4, D], F32R)
        ah = sb("ah", [P, 2, T], F32R)
        al = sb("al", [P, 2, T], F32R)
        g = sb("g", [P, 2, T], F32)
        oneA = sb("oneA", [P, 2 * P * TB // 2], F32)
        iotaA = sb("iotaA", [P, P, TB], F16)
        B = sb("B", [P, 2, TB, 2 * CHUNK], F16)
        E = sb("E", [P, 2, TB, CHUNK], F16)
        lo = sb("lo", [P, 2, TB, CHUNK], F32)
        gh = sb("gh", [P, T], F16)
        gl = sb("gl", [P, T], F16)
        i1 = sb("i1", [P, T], F16)
        i2 = sb("i2", [P, T], F16)
        ident = sb("ident", [P, P], F32)
        ones = sb("ones", [P, P], F32)
        iotaN = sb("iotaN", [P, P], F16)
        gain = sb("gain", [P, 7, DT], F32)
        bank = [ctx.enter_context(nc.psum_tensor(f"bank{b}", [P, 512], F32)) for b in range(8)]

        A = oneA[:, :].bitcast(F16).rearrange("p (s n t) -> p s n t", s=2, t=TB)
        rstd = oneA[:, 0:T]
        a2h, a2l = (v[:, 0:2, :].rearrange("p s n -> p (s n)")[:, 0:2 * T].rearrange("p (k t) -> p k t", k=2)
                    for v in (wh, wl))
        at = [0]

        def arena(*shape, dt=F32):
            n = int(np.prod(shape))
            v = W[:, at[0]:at[0] + n]
            at[0] += n
            assert at[0] <= 2 * CHUNK * T
            v = v if dt == F32 else v.bitcast(dt)
            names = " ".join("abcd"[:len(shape)])
            return v.rearrange(f"p ({names}) -> p {names}", **dict(zip("abcd", shape))) if len(shape) > 1 else v

        uT, vT = arena(DT, T), arena(DT, T)
        vn = arena(NTC, D)
        ws, bsb = arena(GROUPS, P), arena(GROUPS, P)
        at[0] = 0
        qT, kvs = arena(DT, T), arena(4, T)
        vnat, ck, cvs = arena(NTC, KVH * DH), arena(2, P), arena(KVH * DH)
        dst, snk = arena(2 * P), arena(HEADS)
        S = arena(2, 2, 2 * P)
        pT = arena(2, 4, P)
        mx, nm, den, es, rin = (arena(2, 2, 1) for _ in range(5))
        at[0] = 0
        tv = arena(NTC, HP, TOPK)
        ti = arena(NTC, HP, TOPK, dt=U32)
        tif = arena(NTC, HP, TOPK)
        icx = arena(NC * TOPK // 2).bitcast(F16).rearrange("p (c k) -> p c k", k=TOPK)
        first = at[0]
        qs = arena(4, T)
        sk = arena(HP, NK)
        scb = arena(2, NTC, NK)
        scr = arena(NTC, NK)
        at[0] = first
        prod = arena(PH, NC, TOPK)
        eq = arena(PH, NC * TOPK // 2).rearrange("p q n -> p (q n)").bitcast(F16).rearrange(
            "p (q c k) -> p q c k", q=PH, k=TOPK)
        cand, ce, cr = (arena(PH, NC) for _ in range(3))
        bv, ex, gt, es2, f1, f2 = (arena(PH, TOPK) for _ in range(6))
        bp, eu, e1, e2 = (arena(PH, TOPK, dt=U32) for _ in range(4))
        bph = arena(PH * TOPK // 2).bitcast(F16).rearrange("p (q k) -> p q k", q=PH)
        sm, rs = arena(PH), arena(PH)

        full = [sem(f"full{b}") for b in range(8)]
        free = [sem(f"free{b}") for b in range(8)]
        raw_in = [sem(f"raw_in{s}") for s in range(4)]
        hi_done = [sem(f"hi_done{s}") for s in range(4)]
        lo_done = [sem(f"lo_done{s}") for s in range(4)]
        consts_in, sample_in, attn_in, sk_in, x_in, icn_in = (sem(n) for n in (
            "consts_in", "sample_in", "attn_in", "sk_in", "x_in", "icn_in"))
        ones_done, ws_masked = sem("ones_done"), sem("ws_masked")
        sq_done, sq_used = sem("sq_done"), sem("sq_used")
        var_done, std_done, rstd_done = sem("var_done"), sem("std_done"), sem("rstd_done")
        nv_done, xh_done, xl_done = sem("nv_done"), sem("xh_done"), sem("xl_done")
        vnat_done, mixb_done, mixu_done = sem("vnat_done"), sem("mixb_done"), sem("mixu_done")
        out_done = sem("out_done")
        q_ready, sc_ready, top_step = sem("q_ready"), sem("sc_ready"), sem("top_step")
        top_done, tif_done, ce_done, ce_step, cand_done, sub_done, exp_done, eq_done, pr_done, e_done, sel_done = (
            sem(n) for n in ("top_done", "tif_done", "ce_done", "ce_step", "cand_done", "sub_done", "exp_done",
                             "eq_done", "pr_done", "e_done", "sel_done"))
        gh_done, idx_done = sem("gh_done"), sem("idx_done")
        a_one, b_eq, b_one, lo_ready = sem("a_one"), sem("b_eq"), sem("b_one"), sem("lo_ready")
        prod_done, ah_done, a_done = sem("prod_done"), sem("ah_done"), sem("a_done")
        mx_done, nm_done, p_done, es_done, den_done, rin_done, pn_done, oh_done = (
            sem(n) for n in ("mx_done", "nm_done", "p_done", "es_done", "den_done", "rin_done",
                             "pn_done", "oh_done"))
        h_step = sem("h_step")
        spilled, g_in = [sem(f"spilled{t}") for t in range(2)], sem("g_in")

        HALF = [slice(0, TH), slice(TH, T)]
        TCO = [128 * c for c in range(NTC)]
        block = ctx.enter_context(nc.Block())

        UNITS = [(j, c) for j in range(DT) for c in range(NTC)]

        def keys(c):
            return (P, [P]) if c == 0 else (0, [P, P]) if c < 4 else (0, [P, DEC])

        @block.sync
        def _(sp):
            def load(s, src, k):
                sp.wait_ge(lo_done[s], k + 1)
                sp.dma_start(raw[:, s, :], src).then_inc(raw_in[s], 16)

            def linear(name):
                with sp.Fori(0, LIN[name] // 4) as r:
                    for s in range(4):
                        load(s, lin[bass.ds(r * 4 + T0[name] + s, 1), :, :].rearrange("a p n -> p (a n)"),
                             r + KB[name])

            def piece(l, i, s):
                n = (i + l * NPAIR) * 4 + s
                return uv[bass.ds(n, 1), :, :].rearrange("a p n -> p (a n)")

            def experts(l):
                kb, base = KB[f"peer{l}"], BASE[f"peer{l}"]

                def u_load(k, i):
                    for s in (0, 1):
                        load(s, piece(l, i, s), k + kb)

                def v_load(i):
                    for s in (2, 3):
                        load(s, piece(l, i, s), i + kb)

                def park(k, loads):
                    n = k + AHEAD * l if isinstance(k, int) else sp.snap(k + AHEAD * l)
                    for t in range(2):
                        sp.wait_ge(free[1], k * 2 + (base[1] + t + 1))
                        sp.dma_start(parked[bass.ds(n, 1), :, t, :].rearrange("a p n -> p (a n)"),
                                     g[:, t, :]).then_inc(spilled[t], 16)
                        load(t, piece(l, loads[1], t), loads[0] + kb)

                def fetch(i):
                    n = i + (AHEAD * l - MAIN)
                    n = n if isinstance(i, int) else sp.snap(n)
                    sp.wait_ge(a_done, i * 4 + 4 * NPAIR * l)
                    sp.dma_start(g[:, :, :], parked[bass.ds(n, 1), :, :, :].rearrange(
                        "a p t n -> p (a t) n")).then_inc(g_in, 16)

                u_load(0, MAIN)
                u_load(1, MAIN + 1)
                with sp.Fori(0, AHEAD - 2) as k:
                    park(k, (k + 2, k + (MAIN + 2)))
                for k in (AHEAD - 2, AHEAD - 1):
                    park(k, (k + 2, k + 2 - AHEAD))
                with sp.Fori(0, MAIN - 2) as i:
                    v_load(i)
                    u_load(i + (AHEAD + 2), i + 2)
                v_load(MAIN - 2)
                v_load(MAIN - 1)
                for t in range(2):
                    sp.wait_ge(spilled[t], 16 * AHEAD * (l + 1))
                fetch(MAIN)
                with sp.Fori(MAIN, NPAIR - 1) as i:
                    v_load(i)
                    fetch(i + 1)
                v_load(NPAIR - 1)

            for dt in range(DT):
                sp.dma_start(h[:, dt, :], xT[:, dt, :]).then_inc(x_in, 16)
            for name in ("in", "out", "pq0"):
                linear(name)
            experts(0)
            for name in ("kv", "q", "o", "pq1"):
                linear(name)
            experts(1)
            for dt in range(DT):
                sp.wait_ge(nv_done, 6 * DT + dt + 1)
                sp.dma_start(yT[:, dt, :], h[:, dt, :]).then_inc(out_done, 16)
            sp.wait_ge(out_done, 16 * (6 + DT))

        @block.tensor
        def _(pe):
            def product(b, n, cols, terms, width=TH):
                pe.wait_ge(free[b], n)
                for t, (ahi, alo, bhi, blo) in enumerate(terms):
                    pe.matmul(cols, ahi, bhi, start=(t == 0), stop=False)
                    pe.matmul(cols, ahi, blo, start=False, stop=False)
                    mm = pe.matmul(cols, alo, bhi, start=False, stop=(t == len(terms) - 1))
                mm.then_inc(full[b], 1)

            def linear(name):
                with pe.Fori(0, LIN[name] // 4) as r:
                    for s in range(4):
                        pe.wait_ge(lo_done[s], r + (KB[name] + 2))
                        for half in range(2):
                            b = 2 * (s % 2) + half
                            product(b, r * 2 + (BASE[name][b] + s // 2), bank[b][:, 0:TH],
                                    [(wh[:, s, P * k:P * k + P], wl[:, s, P * k:P * k + P],
                                      xh[:, k, HALF[half]], xl[:, k, HALF[half]]) for k in range(DT)])

            def norm_sums(n):
                name = f"n{n}"
                for half in range(2):
                    pe.wait_ge(free[1 + 2 * half], BASE[name][1 + 2 * half])
                for dt in range(DT):
                    pe.wait_ge(sq_done, DT * n + dt + 1)
                    for half in range(2):
                        mm = pe.matmul(bank[1 + 2 * half][:, 0:TH], ones[:, :], g[:, dt % 2, HALF[half]],
                                       start=(dt == 0), stop=(dt == DT - 1))
                        if dt == DT - 1:
                            mm.then_inc(full[1 + 2 * half], 1)
                        elif half == 1:
                            mm.then_inc(sq_used, 1)

            def x_ready(n):
                pe.wait_ge(xh_done, DT * n)
                pe.wait_ge(xl_done, DT * n)

            def selection(l):
                name, bs_ = f"pq{l}", BASE[f"sc{l}"]
                pe.wait_ge(sk_in, 16 * (l + 1))

                def lin_tile(r, s):
                    pe.wait_ge(lo_done[s], r + (KB[name] + 2))
                    for half in range(2):
                        b = 2 * (s % 2) + half
                        product(b, r * 2 + (BASE[name][b] + s // 2), bank[b][:, 0:TH],
                                [(wh[:, s, P * k:P * k + P], wl[:, s, P * k:P * k + P],
                                  xh[:, k, HALF[half]], xl[:, k, HALF[half]]) for k in range(DT)])

                def scores(r, s):
                    pe.wait_ge(q_ready, r * 8 + (HP * 2 * l + 2 * s + 2))
                    for b in (4 + 2 * (s % 2), 5 + 2 * (s % 2)):
                        pe.wait_ge(free[b], r * 2 + (bs_[b] + s // 2))
                    for b, tcs in ((4 + 2 * (s % 2), range(4)), (5 + 2 * (s % 2), [4])):
                        for j, c in enumerate(tcs):
                            mm = pe.matmul(bank[b][0:TCS[c], P * j:P * j + P],
                                           qs[:, s, TCO[c]:TCO[c] + TCS[c]],
                                           sk[:, bass.ds(r * 4 + s, 1), :].rearrange("p a n -> p (a n)"),
                                           start=(j == 0), stop=True, skip_group_check=True)
                        mm.then_inc(full[b], 1)

                with pe.Fori(0, HP // 4) as r:
                    lin_tile(r, 0)
                    for s in (1, 2, 3):
                        lin_tile(r, s)
                        scores(r, s - 1)
                    scores(r, 3)
            def turn(l, c):
                b = 4 + c % 2
                pe.wait_ge(sel_done, NTC * l + c + 1)
                pe.wait_ge(free[b], BASE[f"gt{l}"][b] + c // 2)
                for j, src in enumerate((gt, f1, f2)):
                    mm = pe.transpose(bank[b][:, P * j:P * j + TCS[c]],
                                      src[0:TCS[c], :, :].rearrange("p a b -> p (a b)"),
                                      ident[0:TCS[c], 0:TCS[c]])
                mm.then_inc(full[b], 1)

            def build(l, step, b):
                n = BASE[f"bld{l}"][6 + b % 2] + b // 2
                pe.wait_ge(a_one, step * NB + (NPAIR * NB * l + b + 1))
                pe.wait_ge(b_one, step * NB + (NPAIR * NB * l + b + 1))
                pe.wait_ge(free[6 + b % 2], step * (NB // 2) + n)
                for t in range(TB):
                    mm = pe.matmul(bank[6 + b % 2][:, 2 * CHUNK * t:2 * CHUNK * (t + 1)], A[:, b % 2, :, t],
                                   B[:, b % 2, t, :], start=(t == 0), stop=True, skip_group_check=True)
                mm.then_inc(full[6 + b % 2], 1)

            def expert_scores(l, k, step=None, after=()):
                for u in range(4):
                    t, half = u // 2, u % 2
                    pe.wait_ge(lo_done[t], k + (KB[f"peer{l}"] + 2))
                    product(half, k * 2 + (BASE[f"peer{l}"][half] + t), bank[half][:, 0:TH],
                            [(wh[:, t, P * d:P * d + P], wl[:, t, P * d:P * d + P],
                              xh[:, d, HALF[half]], xl[:, d, HALF[half]]) for d in range(DT)])
                    for b in [b for b, v in enumerate(after) if v == u]:
                        build(l, step, b)

            def expert_sums(l, i, step=None, after=(), b0=0, a=(ah, al)):
                pe.wait_ge(a_done, i * 4 + (4 * NPAIR * l + 4))
                for u in range(2 * DT):
                    d, half = u // 2, u % 2
                    if u in (0, DT):
                        pe.wait_ge(lo_done[2 + u // DT], i + (KB[f"peer{l}"] + 2))
                    s, o, b = 2 + d // 4, P * (d % 4), 2 + u % 4
                    product(b, i * 4 + (BASE[f"peer{l}"][b] + u // 4), bank[b][:, 0:TH],
                            [(wh[:, s, 512 * k + o:512 * k + o + P], wl[:, s, 512 * k + o:512 * k + o + P],
                              a[0][:, k, HALF[half]], a[1][:, k, HALF[half]]) for k in range(2)])
                    if u in after:
                        build(l, step, b0 + after.index(u))

            def experts(l):
                for c in range(4):
                    expert_scores(l, 2 * c)
                    if c >= 1:
                        turn(l, c - 1)
                    expert_scores(l, 2 * c + 1)
                turn(l, 3)
                turn(l, 4)
                with pe.Fori(0, STEPS) as step:
                    expert_scores(l, step + STEPS, step, FIRST_AFTER)
                expert_scores(l, AHEAD)
                with pe.Fori(0, MAIN - 1) as i:
                    expert_scores(l, i + (AHEAD + 1), i + STEPS, SCORES_AFTER)
                    expert_sums(l, i, i + STEPS, SUMS_AFTER, 3)

                def alone(i, odd, building):
                    if building:
                        for b in range(2):
                            build(l, i + STEPS, b)
                    expert_sums(l, i, i + STEPS, ALONE_AFTER if building else (), 2, (ah, al) if odd else (a2h, a2l))

                alone(MAIN - 1, True, True)
                with pe.Fori(0, STEPS // 2 - 1) as j:
                    for e in range(2):
                        alone(j * 2 + (MAIN + e), e == 1, True)
                for e in range(2):
                    alone(NPAIR - STEPS - 2 + e, e == 1, True)
                with pe.Fori(0, STEPS // 2) as j:
                    for e in range(2):
                        alone(j * 2 + (NPAIR - STEPS + e), e == 1, False)

            for b in range(8):
                pe.nop().then_inc(full[b], 1)
            pe.wait_ge(consts_in, 16 * 4)
            pe.wait_ge(ones_done, 1)
            norm_sums(0)
            x_ready(1)
            linear("in")
            norm_sums(1)
            for c in range(NTC):
                for q in range(2):
                    b = 4 + q
                    pe.wait_ge(free[b], BASE["vtr"][b] + c)
                    for k in range(4):
                        dt = 4 * q + k
                        pe.wait_ge(nv_done, DT + dt + 1)
                        mm = pe.transpose(bank[b][0:TCS[c], P * k:P * k + P], vT[:, dt, TCO[c]:TCO[c] + TCS[c]],
                                          ident[:, :])
                    mm.then_inc(full[b], 1)
            pe.wait_ge(vnat_done, 2 * NTC)
            pe.wait_ge(ws_masked, 1)
            for q in range(GROUPS):
                for b, tcs in ((4 + 2 * (q % 2), range(4)), (5 + 2 * (q % 2), [4])):
                    pe.wait_ge(free[b], BASE["mix"][b] + q // 2)
                    for j, c in enumerate(tcs):
                        mm = pe.matmul(bank[b][:, P * j:P * j + TCS[c]], vn[0:TCS[c], c, P * q:P * q + P],
                                       ws[0:TCS[c], q, 0:TCS[c]], start=(j == 0), stop=True, skip_group_check=True)
                    mm.then_inc(full[b], 1)
            x_ready(2)
            linear("out")
            norm_sums(2)
            x_ready(3)
            selection(0)
            experts(0)
            norm_sums(3)
            x_ready(4)
            linear("kv")
            x_ready(5)
            linear("q")
            pe.wait_ge(free[0], BASE["kv"][0] + 2)
            pe.wait_ge(free[1], BASE["kv"][1] + 2)
            pe.wait_ge(free[2], BASE["kv"][2] + 2)
            pe.wait_ge(free[3], BASE["kv"][3] + 2)
            for c in range(NTC):
                b = 6 + c % 2
                pe.wait_ge(free[b], BASE["vn"][b] + c // 2)
                for k in range(2):
                    mm = pe.transpose(bank[b][0:TCS[c], P * k:P * k + P], kvs[:, 2 + k, TCO[c]:TCO[c] + TCS[c]],
                                      ident[:, :])
                mm.then_inc(full[b], 1)

            def att_scores(n):
                j, c = UNITS[n]
                w, k0 = TCS[c], TCO[c]
                for e in range(2):
                    b = n % 2 + 6 * e
                    pe.wait_ge(free[b], BASE["att"][b] + n // 2)
                    r = slice(64 * e, 64 * e + 64)
                    o = 0
                    q = qT[r, j, k0:k0 + w]
                    if c == 0:
                        blocks = [kvs[r, j // 4, 0:P]]
                    elif c < 4:
                        blocks = [kvs[r, j // 4, k0 - P:k0 + P]]
                    else:
                        blocks = [ck[r, j // 4, :], kvs[r, j // 4, k0:k0 + w]]
                    for m, kk in enumerate(blocks):
                        wk = kk.shape[-1]
                        mm = pe.matmul(bank[b][0:w, o:o + wk], q, kk, start=(m == 0), stop=True,
                                       skip_group_check=True)
                        o += wk
                    mm.then_inc(full[b], 1)

            def att_turn(n):
                j, c = UNITS[n]
                w = TCS[c]
                pe.wait_ge(pn_done, 2 * n + 2)
                pe.wait_ge(free[2 + n % 2], BASE["att"][2 + n % 2] + n // 2)
                for e in range(2):
                    o = 0
                    for m, wk in enumerate(keys(c)[1]):
                        mm = pe.transpose(bank[2 + n % 2][0:wk, P * (2 * e + m):P * (2 * e + m) + w],
                                          S[0:w, n % 2, e, o:o + wk], ident[0:w, 0:w])
                        o += wk
                mm.then_inc(full[2 + n % 2], 1)

            def att_out(n):
                j, c = UNITS[n]
                w = TCS[c]
                pe.wait_ge(free[2 + n % 2], BASE["att"][2 + n % 2] + n // 2 + 1)
                pe.wait_ge(free[4 + n % 2], BASE["att"][4 + n % 2] + n // 2)
                for e in range(2):
                    kv = 2 * (j // 4) + e
                    cols = slice(DH * kv, DH * kv + DH)
                    if c == 0:
                        blocks = [vnat[:, 0, cols]]
                    elif c < 4:
                        blocks = [vnat[:, c - 1, cols], vnat[:, c, cols]]
                    else:
                        blocks = [cvs[:, cols], vnat[0:DEC, 4, cols]]
                    for m, vv in enumerate(blocks):
                        wk = keys(c)[1][m]
                        mm = pe.matmul(bank[4 + n % 2][64 * e:64 * e + 64, 0:w], vv, pT[0:wk, n % 2, 2 * e + m, 0:w],
                                       start=(m == 0), stop=(m == len(blocks) - 1), skip_group_check=True)
                mm.then_inc(full[4 + n % 2], 1)

            pe.wait_ge(attn_in, 16 * 4)
            pe.wait_ge(vnat_done, 3 * NTC)
            for b in range(4):
                pe.wait_ge(free[b], BASE["q"][b] + 4)
            for n in range(len(UNITS) + 2):
                if n < len(UNITS):
                    att_scores(n)
                if 0 <= n - 1 < len(UNITS):
                    att_turn(n - 1)
                if 0 <= n - 2:
                    att_out(n - 2)
            for b in (4, 5):
                pe.wait_ge(free[b], BASE["att"][b] + len(UNITS) // 2)
            linear("o")
            norm_sums(4)
            x_ready(6)
            selection(1)
            experts(1)
            norm_sums(5)

        @block.scalar
        def _(act):
            def squares(n, src):
                for dt in range(DT):
                    if dt >= 2:
                        act.wait_ge(sq_used, (DT - 1) * n + dt - 1)
                    act.activation(g[:, dt % 2, :], src[:, dt, :], ACT.Square).then_inc(sq_done, 1)
                for half in range(2):
                    act.wait_ge(var_done, 2 * n + half + 1)
                    act.activation(rstd[:, HALF[half]], rstd[:, HALF[half]], ACT.Sqrt).then_inc(std_done, 1)

            def high_parts(k, n):
                for dt in range(DT):
                    act.wait_ge(nv_done, DT * n + dt + 1)
                    act.activation(xh[:, dt, :], g[:, dt % 2, :], ACT.Copy).then_inc(xh_done, 1)

            def evacuate(name, fn):
                with act.Fori(0, LIN[name] // 4) as r:
                    for s in range(4):
                        for half in range(2):
                            b = 2 * (s % 2) + half
                            act.wait_ge(full[b], r * 2 + (BASE[name][b] + s // 2 + 1))
                            fn(r, s, half, b).then_inc(free[b], 1)

            def at_tile(buf, n, half):
                return buf.rearrange("p a t -> p (a t)")[:, bass.ds(n * T + TH * half, TH)]

            def high(s, k, used):
                act.wait_ge(raw_in[s], k * 16 + 16)
                act.wait_ge(full[used[0]], used[1])
                act.activation(wh[:, s, :], raw[:, s, :], ACT.Copy).then_inc(hi_done[s], 1)

            def selection(l):
                act.wait_ge(xh_done, DT * (3 + 3 * l))
                act.wait_ge(out_done, 16 * 3 * (l + 1))
                if l == 1:
                    act.wait_ge(h_step, 2 * 16)
                act.dma_start(sk, skT[l]).then_inc(sk_in, 16)
                act.dma_start(icx, iota_c).then_inc(icn_in, 16)

                def copy_scores(m):
                    s = m % 4
                    if m >= 2:
                        act.wait_ge(top_done, HP * l + m - 1)
                    for b, lo_, n, c0 in ((4 + 2 * (s % 2), P, 4, 0), (5 + 2 * (s % 2), DEC, 1, 4)):
                        act.wait_ge(full[b], BASE[f"sc{l}"][b] + m // 2 + 1)
                        act.activation(scb[0:lo_, m % 2, c0:c0 + n, :],
                                       bank[b][0:lo_, 0:P * n].rearrange("p (c n) -> p c n", c=n),
                                       ACT.Copy).then_inc(free[b], 1)

                name = f"pq{l}"

                def weight_high(m):
                    s, b = m % 4, 2 * (m % 2) + 1
                    act.wait_ge(raw_in[s], 16 * (KB[name] + m // 4 + 1))
                    act.wait_ge(full[b], BASE[name][b] + m // 2 - 1)
                    act.activation(wh[:, s, :], raw[:, s, :], ACT.Copy).then_inc(hi_done[s], 1)

                for m in range(4):
                    weight_high(m)
                for m in range(HP):
                    if m >= 4:
                        act.wait_ge(full[5 + 2 * (m % 2)], BASE[f"sc{l}"][5 + 2 * (m % 2)] + m // 2 - 1)
                    for half in range(2):
                        b = 2 * (m % 2) + half
                        act.wait_ge(full[b], BASE[name][b] + m // 2 + 1)
                        act.activation(qs[:, m % 4, HALF[half]], bank[b][:, 0:TH], ACT.Copy).then_inc(q_ready, 1)
                    for half in range(2):
                        act.wait_ge(q_ready, 2 * (HP * l + m) + half + 1)
                        act.nop().then_inc(free[2 * (m % 2) + half], 1)
                    if m >= 1:
                        copy_scores(m - 1)
                    if m + 4 < HP:
                        weight_high(m + 4)
                copy_scores(HP - 1)
            def gates_high(l, c):
                b = 4 + c % 2
                act.wait_ge(full[b], BASE[f"gt{l}"][b] + c // 2 + 1)
                act.activation(gh[:, TCO[c]:TCO[c] + TCS[c]], bank[b][:, 0:TCS[c]], ACT.Copy,
                               scale=GS).then_inc(gh_done, 1)

            def gate_exp(l, c):
                act.wait_ge(sub_done, NTC * l + c + 1)
                act.activation(ex[0:TCS[c]], ex[0:TCS[c]], ACT.Exp).then_inc(exp_done, 1)

            def build(l, step, b):
                act.wait_ge(full[6 + b % 2], step * (NB // 2) + (BASE[f"bld{l}"][6 + b % 2] + b // 2 + 1))
                act.wait_ge(free[6 + b % 2], step * (NB // 2) + (BASE[f"bld{l}"][6 + b % 2] + b // 2))
                act.activation(lo[:, b % 2, :, :],
                               bank[6 + b % 2][:, 0:2 * CHUNK * TB].rearrange("p (t n) -> p t n", t=TB)[:, :, CHUNK:],
                               ACT.Copy, scale=1.0 / GS).then_inc(lo_ready, 1)

            def experts(l):
                kb, base = KB[f"peer{l}"], BASE[f"peer{l}"]

                def u_high(k, t):
                    high(t, k + kb, (1, k * 2 + (base[1] + t - 1)))

                def v_high(i):
                    for s in (2, 3):
                        high(s, i + kb, (5, i * 4 + (base[5] if s == 3 else base[5] - 2)))

                def score_step(k, parked_=False, first=False, last=False, step=None, after=()):
                    for u in range(4):
                        t, half = u // 2, u % 2
                        act.wait_ge(full[half], k * 2 + (base[half] + t + 1))
                        if parked_:
                            act.wait_ge(spilled[t], k * 16 + 16 * AHEAD * l)
                        elif not first:
                            act.wait_ge(a_done, k * 4 + (4 * NPAIR * l - 4 * (AHEAD + 1) + u + 1))
                        act.activation(g[:, t, HALF[half]], bank[half][:, 0:TH],
                                       ACT.Gelu_apprx_tanh).then_inc(free[half], 1)
                        if u % 2 == 1 and not last:
                            u_high(k + 1, t)
                        for b in [b for b, v in enumerate(after) if v == u]:
                            build(l, step, b)

                for t in range(2):
                    high(t, kb, (2 * t + 1, base[2 * t + 1]))
                for c in range(4):
                    score_step(2 * c, parked_=c > 0, first=c == 0)
                    gate_exp(l, c)
                    if c >= 1:
                        gates_high(l, c - 1)
                    score_step(2 * c + 1, parked_=True)
                gate_exp(l, 4)
                gates_high(l, 3)
                gates_high(l, 4)
                with act.Fori(0, STEPS) as step:
                    score_step(step + STEPS, parked_=True, step=step, after=FIRST_AFTER)
                score_step(AHEAD, parked_=True)
                with act.Fori(0, MAIN - 2) as i:
                    v_high(i)
                    score_step(i + (AHEAD + 1), step=i + STEPS, after=SCORES_AFTER)
                    for b in range(3, NB):
                        build(l, i + STEPS, b)
                i = MAIN - 2
                v_high(i)
                score_step(i + AHEAD + 1, last=True, step=i + STEPS, after=SCORES_AFTER)
                for b in range(3, NB):
                    build(l, i + STEPS, b)
                with act.Fori(MAIN - 1, NPAIR - STEPS) as i:
                    v_high(i)
                    for b in range(NB):
                        build(l, i + STEPS, b)
                with act.Fori(NPAIR - STEPS, NPAIR) as i:
                    v_high(i)

            act.dma_start(ident[:, :], ident_c).then_inc(consts_in, 16)
            act.dma_start(gain[:, :, :], gains).then_inc(consts_in, 16)
            act.dma_start(iotaA[:, :, :], iota_a).then_inc(consts_in, 16)
            act.dma_start(iotaN[:, :], iota_n).then_inc(consts_in, 16)
            act.dma_start(ws, wsT).then_inc(sample_in, 16)
            act.dma_start(bsb, bs.broadcast_to([P, GROUPS, P])).then_inc(sample_in, 16)
            act.dma_start(kwin[:, :, 0:DEC], ckT[:, :, DEC:P]).then_inc(out_done, 16)
            act.dma_start(vwin[0:DEC, :], cv[DEC:P, :]).then_inc(out_done, 16)

            act.wait_ge(x_in, 16 * DT)
            squares(0, h)
            high_parts(0, 0)
            uv_all = W[:, 0:2 * DT * T]
            evacuate("in", lambda r, s, half, b: act.activation(
                uv_all[:, bass.ds(r * (4 * T) + (T * s + TH * half), TH)], bank[b][:, 0:TH], ACT.Gelu_apprx_tanh))
            for b in range(4):
                act.wait_ge(free[b], BASE["in"][b] + 8)
            squares(1, vT)
            for c in range(NTC):
                act.wait_ge(full[4], BASE["vtr"][4] + c + 1)
                act.activation(vn[0:TCS[c], c, 0:512], bank[4][0:TCS[c], :], ACT.Copy).then_inc(free[4], 1)
            act.wait_ge(free[4], BASE["vtr"][4] + NTC)
            act.wait_ge(vnat_done, 2 * NTC)
            act.dma_start(gv, vn[0:DEC, 4, :]).then_inc(out_done, 16)
            for q in range(GROUPS):
                act.wait_ge(mixu_done, q + 1)
                act.activation(xh[:, q, :], vT[:, q, :], ACT.Copy).then_inc(xh_done, 1)
            def weights_high(name):
                with act.Fori(0, LIN[name] // 4) as r:
                    for s in range(4):
                        high(s, r + KB[name], (2 * (s % 2) + 1, r * 2 + (BASE[name][2 * (s % 2) + 1] + s // 2 - 1)))

            weights_high("out")
            act.wait_ge(h_step, 16)
            squares(2, h)
            high_parts(2, 2)
            selection(0)
            experts(0)
            for b in range(2, 6):
                act.wait_ge(free[b], BASE["peer0"][b] + 4 * NPAIR)
            act.dma_start(ck, ckT).then_inc(attn_in, 16)
            act.dma_start(cvs, cv).then_inc(attn_in, 16)
            act.dma_start(dst, dist).then_inc(attn_in, 16)
            act.dma_start(snk, sinks.broadcast_to([P, HEADS])).then_inc(attn_in, 16)
            squares(3, h)
            high_parts(3, 3)
            evacuate("kv", lambda r, s, half, b: act.activation(kvs[:, s, HALF[half]], bank[b][:, 0:TH], ACT.Copy))
            high_parts(4, 4)
            evacuate("q", lambda r, s, half, b: act.activation(
                qT.rearrange("p a t -> p (a t)")[:, bass.ds(r * (4 * T) + (T * s + TH * half), TH)],
                bank[b][:, 0:TH], ACT.Copy, scale=DH ** -0.5))
            for b in range(4):
                act.wait_ge(free[b], BASE["kv"][b] + 2)
            act.dma_start(kvT, kvs[:, :, SEQ - P:SEQ]).then_inc(out_done, 16)
            act.dma_start(kwin[:, :, DEC:P], kvs[:, 0:2, SEQ:T]).then_inc(out_done, 16)
            act.wait_ge(vnat_done, 3 * NTC)
            act.dma_start(vwin[DEC:P, :], vnat[0:DEC, 4, :]).then_inc(out_done, 16)
            act.wait_ge(attn_in, 16 * 4)

            def att_exp(n):
                j, c = UNITS[n]
                w, wk = TCS[c], sum(keys(c)[1])
                for e in range(2):
                    hd = 4 * (2 * (j // 4) + e) + j % 4
                    act.wait_ge(nm_done, 2 * n + e + 1)
                    act.activation(S[0:w, n % 2, e, 0:wk], S[0:w, n % 2, e, 0:wk], ACT.Exp,
                                   bias=nm[0:w, n % 2, e, :], accum_out=den[0:w, n % 2, e, :]).then_inc(p_done, 1)
                    act.activation(es[0:w, n % 2, e, :], snk[0:w, hd:hd + 1], ACT.Exp,
                                   bias=nm[0:w, n % 2, e, :]).then_inc(es_done, 1)

            def att_copy(n):
                j, c = UNITS[n]
                w, wks = TCS[c], keys(c)[1]
                act.wait_ge(full[2 + n % 2], BASE["att"][2 + n % 2] + n // 2 + 1)
                if n >= 2:
                    act.wait_ge(full[4 + n % 2], BASE["att"][4 + n % 2] + n // 2)
                if wks == [P, P]:
                    act.activation(pT[:, n % 2, :, :], bank[2 + n % 2][:, :].rearrange("p (a q) -> p a q", a=4),
                                   ACT.Copy).then_inc(free[2 + n % 2], 1)
                    return
                src = bank[2 + n % 2][:, :].rearrange("p (e m q) -> p e m q", e=2, m=2)
                dstp = pT[:, n % 2, :, :].rearrange("p (e m) q -> p e m q", e=2)
                for m, wk in enumerate(wks):
                    a = act.activation(dstp[0:wk, :, m, 0:w], src[0:wk, :, m, 0:w], ACT.Copy)
                a.then_inc(free[2 + n % 2], 1)

            def att_high(n):
                j, c = UNITS[n]
                act.wait_ge(full[4 + n % 2], BASE["att"][4 + n % 2] + n // 2 + 1)
                act.activation(xh[:, j, TCO[c]:TCO[c] + TCS[c]], bank[4 + n % 2][:, 0:TCS[c]],
                               ACT.Copy).then_inc(oh_done, 1)

            for n in range(len(UNITS) + 2):
                if n < len(UNITS):
                    att_exp(n)
                if 0 <= n - 1 < len(UNITS):
                    att_copy(n - 1)
                if 0 <= n - 2:
                    att_high(n - 2)
            weights_high("o")
            act.wait_ge(h_step, 2 * 16)
            squares(4, h)
            high_parts(5, 5)
            selection(1)
            experts(1)
            for b in range(2, 6):
                act.wait_ge(free[b], BASE["peer1"][b] + 4 * NPAIR)
            squares(5, h)

        @block.gpsimd
        def _(pool):
            def low(s, k):
                pool.wait_ge(hi_done[s], k + 1)
                pool.tensor_tensor(wl[:, s, :], raw[:, s, :], wh[:, s, :].bitcast(F32),
                                   ALU.subtract).then_inc(lo_done[s], 1)

            def weights_low(name):
                with pool.Fori(0, LIN[name] // 4) as r:
                    for s in range(4):
                        low(s, r + KB[name])

            def low_parts(k):
                for dt in range(DT):
                    pool.wait_ge(xh_done, DT * k + dt + 1)
                    pool.tensor_tensor(xl[:, dt, :], g[:, dt % 2, :], xh[:, dt, :].bitcast(F32),
                                       ALU.subtract).then_inc(xl_done, 1)

            def selection(l):
                weights_low(f"pq{l}")
                kb = KB[f"peer{l}"]
                low(0, kb)
                low(1, kb)
                pool.wait_ge(top_done, HP * (l + 1))

                def sums(c):
                    n = TCS[c]
                    f = tif[0:n, c, :, :].rearrange("p (h two) k -> p h two k", two=2)
                    t = ti[0:n, c, :, :].rearrange("p (h two) k -> p h two k", two=2)
                    pool.tensor_scalar(f[:, :, 0, :], t[:, :, 0, :], float(NK), None, ALU.mult)
                    pool.tensor_copy(f[:, :, 1, :], t[:, :, 1, :]).then_inc(tif_done, 1)
                    pool.wait_ge(tif_done, NTC * l + c + 1)
                    if c >= 1:
                        pool.wait_ge(e_done, NTC * l + c)
                    for a in range(TOPK // 2):
                        pool.tensor_tensor(ce[0:n, :, OFFS[a]:OFFS[a] + ROWS[a]],
                                           f[:, :, 0, a:a + 1].broadcast_to([n, PH, ROWS[a]]),
                                           f[:, :, 1, 0:ROWS[a]], ALU.add)
                    pool.tensor_tensor(ce[0:n, :, OFFS[-1]:NC], f[:, :, 0, TOPK // 2:TOPK],
                                       f[:, :, 1, 0:1].broadcast_to([n, PH, TOPK // 2]),
                                       ALU.add).then_inc(ce_done, 1)
                    pool.wait_ge(ce_done, NTC * l + c + 1)

                for c in range(NTC):
                    n = TCS[c]
                    sums(c)
                    for q in range(POOLED):
                        pool.wait_ge(eq_done, PH * (NTC * l + c) + q + 1)
                        pool.tensor_tensor(prod[0:n, q], eq[0:n, q], ce[0:n, q, :, None].broadcast_to([n, NC, TOPK]),
                                           ALU.mult).then_inc(pr_done, 1)
                        if q in (1, 3, 5) and c < 4:
                            j = 4 * c + (q - 1) // 2
                            low(j % 2, kb + 1 + j // 2)
                    if c < 3:
                        low(1, kb + 2 + 2 * c)

            def build(l, step, b, tok):
                pool.wait_ge(full[6 + b % 2], step * (NB // 2) + (BASE[f"bld{l}"][6 + b % 2] + b // 2))
                pool.wait_ge(b_eq, step * NB + (NPAIR * NB * l + b + 1))
                pool.tensor_tensor(B[:, b % 2, :, 0:CHUNK], E[:, b % 2],
                                   gh[:, bass.ds(tok, TB)][:, :, None].broadcast_to([P, TB, CHUNK]), ALU.mult)
                pool.tensor_tensor(B[:, b % 2, :, CHUNK:], E[:, b % 2],
                                   gl[:, bass.ds(tok, TB)][:, :, None].broadcast_to([P, TB, CHUNK]),
                                   ALU.mult).then_inc(b_one, 1)

            def experts(l):
                kb = KB[f"peer{l}"]

                def splits(i):
                    low(2, i + kb)
                    low(3, i + kb)

                pool.wait_ge(idx_done, NTC * (l + 1))
                with pool.Fori(0, STEPS) as step:
                    for b in range(NB):
                        build(l, step, b, step * (TB * NB) + TB * b)
                        if b == 1:
                            low(1, step + (kb + STEPS))
                        elif b == 3:
                            low(0, step + (kb + STEPS + 1))
                low(1, kb + AHEAD)
                low(0, kb + AHEAD + 1)
                low(1, kb + AHEAD + 1)
                with pool.Fori(0, MAIN - 2) as i:
                    tok = (i % STEPS) * (TB * NB)
                    for b in range(NB):
                        build(l, i + STEPS, b, tok + TB * b)
                        if b == 1:
                            splits(i)
                        elif b in (2, 3):
                            low(b - 2, i + (kb + AHEAD + 2))
                with pool.Fori(MAIN - 2, NPAIR - STEPS) as i:
                    tok = (i % STEPS) * (TB * NB)
                    for b in range(NB):
                        build(l, i + STEPS, b, tok + TB * b)
                        if b == 1:
                            splits(i)
                with pool.Fori(NPAIR - STEPS, NPAIR) as i:
                    splits(i)

            for s in range(4):
                pool.nop().then_inc(lo_done[s], 1)
            pool.memset(ones[:, :], 1.0).then_inc(ones_done, 1)
            pool.wait_ge(ones_done, 1)
            pool.wait_ge(sample_in, 16 * 2)
            pool.memset(ws[64:P, :, 0:64], 0.0).then_inc(ws_masked, 1)
            pool.wait_ge(ws_masked, 1)
            low_parts(0)
            weights_low("in")
            for q in range(GROUPS):
                pool.wait_ge(xh_done, DT + q + 1)
                pool.tensor_tensor(xl[:, q, :], vT[:, q, :], xh[:, q, :].bitcast(F32), ALU.subtract)\
                    .then_inc(xl_done, 1)
            weights_low("out")
            low_parts(2)
            selection(0)
            experts(0)
            low_parts(3)
            weights_low("kv")
            low_parts(4)
            weights_low("q")
            weights_low("o")
            low_parts(5)
            selection(1)
            experts(1)

        @block.vector
        def _(dve):
            def stats(n):
                for half in range(2):
                    b = 1 + 2 * half
                    dve.wait_ge(full[b], BASE[f"n{n}"][b] + 1)
                    dve.tensor_scalar(rstd[:, HALF[half]], bank[b][:, 0:TH], 1.0 / D, EPS,
                                      ALU.mult, ALU.add).then_inc(var_done, 1)
                for half in range(2):
                    dve.wait_ge(std_done, 2 * n + half + 1)
                    dve.reciprocal(rstd[:, HALF[half]], rstd[:, HALF[half]]).then_inc(rstd_done, 1)
                for half in range(2):
                    b = 1 + 2 * half
                    dve.wait_ge(rstd_done, 2 * n + half + 1)
                    dve.nop().then_inc(free[b], 1)

            def apply(k, gi, src, out, split):
                for dt in range(DT):
                    if split is not None and dt >= 2:
                        dve.wait_ge(xl_done, DT * split + dt - 1)
                    dve.scalar_tensor_tensor(out=out(dt), in0=src[:, dt, :], scalar=gain[:, gi, dt:dt + 1],
                                             in1=rstd, op0=ALU.mult, op1=ALU.mult).then_inc(nv_done, 1)

            def in_g(dt):
                return g[:, dt % 2, :]

            def high(s, k, b, n):
                dve.wait_ge(raw_in[s], k * 16 + 16)
                dve.wait_ge(full[b], n)
                dve.tensor_copy(wh[:, s, :], raw[:, s, :]).then_inc(hi_done[s], 1)

            def weights_high(name):
                with dve.Fori(0, LIN[name] // 4) as r:
                    for s in range(4):
                        b = 2 * (s % 2) + 1
                        high(s, r + KB[name], b, r * 2 + (BASE[name][b] + s // 2 - 1))

            def add_to_h(name):
                hf = h[:, :, :].rearrange("p a t -> p (a t)")
                with dve.Fori(0, LIN[name] // 4) as r:
                    for s in range(4):
                        for half in range(2):
                            b = 2 * (s % 2) + half
                            dve.wait_ge(full[b], r * 2 + (BASE[name][b] + s // 2 + 1))
                            cols = hf[:, bass.ds(r * (4 * T) + (T * s + TH * half), TH)]
                            dve.tensor_tensor(cols, cols, bank[b][:, 0:TH], ALU.add).then_inc(free[b], 1)
                for b in range(4):
                    dve.wait_ge(free[b], BASE[name][b] + LIN[name] // 2)
                dve.nop().then_inc(h_step, 16)

            def search(val, idx, src, spare, shapes, step):
                n = step
                k = len(shapes)
                for j in range(k):
                    dve.max(out=val(j)[:, 0:8], in_=src(j)).then_inc(top_step, 1)
                n += k
                for j in range(k):
                    dve.wait_ge(top_step, n - k + j + 1)
                    dve.max_index(out=idx(j)[:, 0:8], in_max=val(j)[:, 0:8], in_values=src(j)).then_inc(top_step, 1)
                    dve.match_replace(out=spare(j), in_to_replace=val(j)[:, 0:8], in_values=src(j),
                                      imm_value=NEGBIG).then_inc(top_step, 1)
                n += 2 * k
                for j in range(k):
                    dve.wait_ge(top_step, n - 2 * k + 2 * j + 2)
                    dve.max(out=val(j)[:, 8:16], in_=spare(j)).then_inc(top_step, 1)
                n += k
                for j in range(k):
                    dve.wait_ge(top_step, n - k + j + 1)
                    last = dve.max_index(out=idx(j)[:, 8:16], in_max=val(j)[:, 8:16], in_values=spare(j))
                    if j < k - 1:
                        last.then_inc(top_step, 1)
                return n + k - 1, last

            PER = 5 * NTC - 1 + 0

            def selection(l, step):
                for m in range(HP):
                    for b in (4 + 2 * (m % 2), 5 + 2 * (m % 2)):
                        dve.wait_ge(free[b], BASE[f"sc{l}"][b] + m // 2 + 1)
                    if m >= 1:
                        dve.wait_ge(top_done, HP * l + m)
                    step, last = search(lambda c: tv[0:TCS[c], c, m, :], lambda c: ti[0:TCS[c], c, m, :],
                                        lambda c: scb[0:TCS[c], m % 2, c, :], lambda c: scr[0:TCS[c], c, :],
                                        TCS, step)
                    last.then_inc(top_done, 1)
                dve.wait_ge(icn_in, 16 * (l + 1))
                dve.wait_ge(top_done, HP * (l + 1))
                for c in range(NTC):
                    n = TCS[c]
                    v = tv[0:n, c, :, :].rearrange("p (h two) k -> p h two k", two=2)
                    for a in range(TOPK // 2):
                        dve.tensor_tensor(cand[0:n, :, OFFS[a]:OFFS[a] + ROWS[a]],
                                          v[:, :, 0, a:a + 1].broadcast_to([n, PH, ROWS[a]]),
                                          v[:, :, 1, 0:ROWS[a]], ALU.add)
                    dve.tensor_tensor(cand[0:n, :, OFFS[-1]:NC], v[:, :, 0, TOPK // 2:TOPK],
                                      v[:, :, 1, 0:1].broadcast_to([n, PH, TOPK // 2]),
                                      ALU.add).then_inc(cand_done, 1)
                    dve.wait_ge(cand_done, NTC * l + c + 1)
                    step, last = search(lambda q: bv[0:n, q, :], lambda q: bp[0:n, q, :],
                                        lambda q: cand[0:n, q, :], lambda q: cr[0:n, q, :], range(PH), step)
                    last.then_inc(top_step, 1)
                    step += 1
                    dve.wait_ge(top_step, step)
                    dve.tensor_tensor(ex[0:n], bv[0:n], bv[0:n, :, 0:1].broadcast_to([n, PH, TOPK]),
                                      ALU.subtract).then_inc(sub_done, 1)
                    dve.tensor_copy(bph[0:n], bp[0:n]).then_inc(top_step, 1)
                    step += 1
                    dve.wait_ge(top_step, step)
                    for q in range(PH):
                        dve.tensor_tensor(eq[0:n, q], icx[0:n], bph[0:n, q, None, :].broadcast_to([n, NC, TOPK]),
                                          ALU.is_equal).then_inc(eq_done, 1)
                    dve.wait_ge(ce_done, NTC * l + c + 1)
                    for q in range(POOLED, PH):
                        dve.wait_ge(eq_done, PH * (NTC * l + c) + q + 1)
                        dve.tensor_tensor(prod[0:n, q], eq[0:n, q], ce[0:n, q, :, None].broadcast_to([n, NC, TOPK]),
                                          ALU.mult).then_inc(top_step, 1)
                        step += 1
                    for q in [*range(POOLED, PH), *range(POOLED)]:
                        if q >= POOLED:
                            dve.wait_ge(top_step, step - (PH - 1 - q))
                        else:
                            dve.wait_ge(pr_done, POOLED * (NTC * l + c) + q + 1)
                        last = dve.tensor_reduce(es2[0:n, q, :], prod[0:n, q].rearrange("p c k -> p k c"), AX, ALU.add)
                    last.then_inc(e_done, 1)
                    dve.wait_ge(e_done, NTC * l + c + 1)

                    def link(ins):
                        nonlocal step
                        ins.then_inc(top_step, 1)
                        step += 1
                        dve.wait_ge(top_step, step)

                    link(dve.tensor_copy(eu[0:n], es2[0:n]))
                    link(dve.tensor_scalar(e1[0:n], eu[0:n], 7, None, ALU.logical_shift_right))
                    link(dve.tensor_scalar(e2[0:n], eu[0:n], NK - 1, None, ALU.bitwise_and))
                    if c >= 1:
                        dve.wait_ge(full[4 + (c - 1) % 2], BASE[f"gt{l}"][4 + (c - 1) % 2] + (c - 1) // 2 + 1)
                    link(dve.tensor_copy(f1[0:n], e1[0:n]))
                    link(dve.tensor_copy(f2[0:n], e2[0:n]))
                    dve.wait_ge(exp_done, NTC * l + c + 1)
                    link(dve.tensor_reduce(sm[0:n], ex[0:n], AX, ALU.add))
                    link(dve.reciprocal(rs[0:n], sm[0:n]))
                    dve.tensor_tensor(gt[0:n], ex[0:n], rs[0:n, :, None].broadcast_to([n, PH, TOPK]),
                                      ALU.mult).then_inc(sel_done, 1)
                    dve.wait_ge(sel_done, NTC * l + c + 1)
                    if c >= 1:
                        take(l, c - 1)
                take(l, NTC - 1)
                return step

            def take(l, c):
                b, n = 4 + c % 2, TCS[c]
                cols = slice(TCO[c], TCO[c] + n)
                dve.wait_ge(full[b], BASE[f"gt{l}"][b] + c // 2 + 1)
                dve.wait_ge(gh_done, NTC * l + c + 1)
                dve.tensor_copy(i1[:, cols], bank[b][:, P:P + n])
                dve.tensor_copy(i2[:, cols], bank[b][:, 2 * P:2 * P + n])
                dve.scalar_tensor_tensor(out=gl[:, cols], in0=bank[b][:, 0:n], scalar=GS, in1=gh[:, cols],
                                         op0=ALU.mult, op1=ALU.subtract).then_inc(idx_done, 1)
                dve.wait_ge(idx_done, NTC * l + c + 1)
                dve.nop().then_inc(free[b], 1)

            def one_hot(l, step, b):
                tok = (step % STEPS) * (TB * NB) + TB * b
                n2 = (step // STEPS) * CHUNK
                dve.wait_ge(full[6 + b % 2], step * (NB // 2) + (BASE[f"bld{l}"][6 + b % 2] + b // 2))
                dve.tensor_tensor(E[:, b % 2], iotaN[:, bass.ds(n2, CHUNK)][:, None, :].broadcast_to([P, TB, CHUNK]),
                                  i2[:, bass.ds(tok, TB)][:, :, None].broadcast_to([P, TB, CHUNK]),
                                  ALU.is_equal).then_inc(b_eq, 1)
                dve.tensor_tensor(A[:, b % 2], iotaA[:, :, :], i1[:, None, bass.ds(tok, TB)].broadcast_to([P, P, TB]),
                                  ALU.is_equal).then_inc(a_one, 1)

            def to_w(l, step, b, off):
                dve.wait_ge(lo_ready, step * NB + (NPAIR * NB * l + b + 1))
                src = bank[6 + b % 2][:, 0:2 * CHUNK * TB].rearrange("p (t n) -> p n t", t=TB)[:, 0:CHUNK, :]
                dst_ = W3(off)
                dve.scalar_tensor_tensor(out=dst_, in0=src, scalar=1.0 / GS,
                                         in1=lo[:, b % 2, :, :].rearrange("p t n -> p n t"),
                                         op0=ALU.mult, op1=ALU.add).then_inc(free[6 + b % 2], 1)

            def W3(off):
                return W[:, :].rearrange("p (c t) -> p c t", t=T)[:, bass.ds(off[0], CHUNK), bass.ds(off[1], TB)]

            def gate_parts(l, i, built, ahead=False, late=False):
                base = BASE[f"peer{l}"]
                tile = (i % CHUNK) * 2
                Wt = W[:, :].rearrange("p (c t) -> p c t", t=T)
                hi, lw = (a2h, a2l) if late == "even" else (ah, al)

                def products(k):
                    if k == 0:
                        for b in (6, 7):
                            dve.wait_ge(free[b], built + BASE[f"bld{l}"][b])
                        if late:
                            dve.wait_ge(g_in, i * 16 + 16 * (AHEAD * l - MAIN + 1))
                    for half in range(2):
                        if not late:
                            dve.wait_ge(free[half], i * 2 + (base[half] + 2 * AHEAD + k + 1))
                        dve.tensor_tensor(g[:, k, HALF[half]], g[:, k, HALF[half]],
                                          Wt[:, bass.ds(tile + k, 1), HALF[half]].rearrange("p a t -> p (a t)"),
                                          ALU.mult).then_inc(prod_done, 1)

                def highs():
                    dve.wait_ge(full[5], i * 4 + (base[5] - 4 if ahead else base[5]))
                    if late == "even":
                        dve.wait_ge(full[1], base[1] + 2 * NPAIR)
                    for u in range(4):
                        dve.wait_ge(prod_done, i * 4 + (4 * NPAIR * l + u + 1))
                        dve.tensor_copy(hi[:, u // 2, HALF[u % 2]], g[:, u // 2, HALF[u % 2]]).then_inc(ah_done, 1)

                def lows(k):
                    for u in (2 * k, 2 * k + 1):
                        dve.wait_ge(ah_done, i * 4 + (4 * NPAIR * l + u + 1))
                        dve.tensor_tensor(lw[:, k, HALF[u % 2]], g[:, k, HALF[u % 2]],
                                          hi[:, k, HALF[u % 2]].bitcast(F32), ALU.subtract).then_inc(a_done, 1)

                return (lambda: products(0), lambda: products(1), highs, lambda: lows(0), lambda: lows(1))

            def add_sums(l, i, u):
                b, d = 2 + u % 4, u // 2
                dve.wait_ge(full[b], i * 4 + (BASE[f"peer{l}"][b] + u // 4 + 1))
                dve.tensor_tensor(h[:, d, HALF[u % 2]], h[:, d, HALF[u % 2]], bank[b][:, 0:TH],
                                  ALU.add).then_inc(free[b], 1)

            def experts(l):
                one_hot(l, 0, 0)
                one_hot(l, 0, 1)
                with dve.Fori(0, STEPS) as step:
                    for b in range(NB):
                        to_w(l, step, b, (0, step * (TB * NB) + TB * b))
                        one_hot(l, step + (b + 2) // NB, (b + 2) % NB)

                def pair(i, early, after, own=True, ahead=None, building=True):
                    tok = (i % STEPS) * (TB * NB)
                    c0 = ((i // STEPS + 1) % 2) * CHUNK
                    built = (i + STEPS) * (NB // 2) if building else NPAIR * NB // 2

                    def batch(b):
                        to_w(l, i + STEPS, b, (c0, tok + TB * b))
                        step = i + STEPS + (b + 2) // NB
                        if not (isinstance(step, int) and step == NPAIR):
                            one_hot(l, step, (b + 2) % NB)

                    if own:
                        for part in gate_parts(l, i, built):
                            part()
                    parts = {}
                    if ahead:
                        among = ahead[1]
                        todo = gate_parts(l, i + 1, built if among else built + NB // 2 * building, True, ahead[0])
                        parts = dict(zip(GATE_AFTER if among else [None] * 5, todo))
                    if building:
                        for b in range(early):
                            batch(b)
                    for u in range(2 * DT):
                        add_sums(l, i, u)
                        if building and u in after:
                            batch(early + after.index(u))
                        if u in parts:
                            parts[u]()
                    if ahead and not among:
                        for part in todo:
                            part()

                with dve.Fori(0, MAIN - 1) as i:
                    pair(i, 3, SUMS_AFTER)
                kinds = ("odd", "even")
                pair(MAIN - 1, 2, ALONE_AFTER, True, ("even", False))
                with dve.Fori(0, STEPS // 2 - 1) as j:
                    for e in range(2):
                        pair(j * 2 + (MAIN + e), 2, ALONE_AFTER, False, (kinds[e], True))
                pair(NPAIR - STEPS - 2, 2, ALONE_AFTER, False, ("odd", True))
                pair(NPAIR - STEPS - 1, 2, ALONE_AFTER, False, ("even", False))
                with dve.Fori(0, STEPS // 2 - 1) as j:
                    for e in range(2):
                        pair(j * 2 + (NPAIR - STEPS + e), 0, (), False, (kinds[e], True), building=False)
                pair(NPAIR - 2, 0, (), False, ("odd", True), building=False)
                pair(NPAIR - 1, 0, (), False, None, building=False)

            step = 0
            for b in range(8):
                dve.nop().then_inc(free[b], 1)
            dve.wait_ge(consts_in, 16 * 4)
            stats(0)
            apply(0, G_MIX0, h, in_g, 0)
            weights_high("in")
            stats(1)
            apply(1, G_V, vT, lambda dt: vT[:, dt, :], None)
            for c in range(NTC):
                dve.wait_ge(full[5], BASE["vtr"][5] + c + 1)
                dve.tensor_copy(vn[0:TCS[c], c, 512:D], bank[5][0:TCS[c], :]).then_inc(free[5], 1)
            for c in range(2 * NTC):
                if c == 0:
                    dve.wait_ge(free[4], BASE["vtr"][4] + NTC)
                    dve.wait_ge(free[5], BASE["vtr"][5] + NTC)
                    dve.nop().then_inc(vnat_done, 2 * NTC)
            dve.wait_ge(sample_in, 32)
            for q in range(GROUPS):
                ba, bb = 4 + 2 * (q % 2), 5 + 2 * (q % 2)
                dve.wait_ge(full[ba], BASE["mix"][ba] + q // 2 + 1)
                dve.tensor_tensor(vT[:, q, 0:SEQ].rearrange("p (c n) -> p c n", c=4),
                                  bank[ba][:, :].rearrange("p (c n) -> p c n", c=4),
                                  bsb[:, q, None, :].broadcast_to([P, 4, P]), ALU.add).then_inc(free[ba], 1)
                dve.wait_ge(full[bb], BASE["mix"][bb] + q // 2 + 1)
                dve.tensor_tensor(vT[:, q, SEQ:T], bank[bb][:, 0:DEC], bsb[:, q, 0:DEC], ALU.add)\
                    .then_inc(free[bb], 1)
                dve.wait_ge(free[ba], BASE["mix"][ba] + q // 2 + 1)
                dve.wait_ge(free[bb], BASE["mix"][bb] + q // 2 + 1)
                dve.tensor_tensor(vT[:, q, :], vT[:, q, :], uT[:, q, :], ALU.mult).then_inc(mixu_done, 1)
            add_to_h("out")
            stats(2)
            apply(2, G_FFN0, h, in_g, 2)
            step = selection(0, step)
            experts(0)
            stats(3)
            apply(3, G_KV, h, in_g, 3)
            weights_high("kv")
            for b in range(4):
                dve.wait_ge(full[b], BASE["kv"][b] + 2)
            apply(4, G_MIX1, h, in_g, 4)
            weights_high("q")
            for c in range(NTC):
                b = 6 + c % 2
                dve.wait_ge(full[b], BASE["vn"][b] + c // 2 + 1)
                dve.tensor_copy(vnat[0:TCS[c], c, :], bank[b][0:TCS[c], 0:KVH * DH]).then_inc(free[b], 1)
            dve.wait_ge(free[6], BASE["vn"][6] + 3)
            dve.wait_ge(free[7], BASE["vn"][7] + 2)
            dve.nop().then_inc(vnat_done, NTC)
            dve.wait_ge(attn_in, 16 * 4)

            def att_max(n):
                j, c = UNITS[n]
                w, (c0, wks) = TCS[c], keys(c)
                wk = sum(wks)
                if n >= 2:
                    dve.wait_ge(full[2 + n % 2], BASE["att"][2 + n % 2] + n // 2)
                for e in range(2):
                    b = n % 2 + 6 * e
                    dve.wait_ge(full[b], BASE["att"][b] + n // 2 + 1)
                    hd = 4 * (2 * (j // 4) + e) + j % 4
                    slope = 2.0 ** (-8.0 * (hd + 1) / HEADS)
                    dve.scalar_tensor_tensor(out=S[0:w, n % 2, e, 0:wk], in0=dst[0:w, c0:c0 + wk], scalar=-slope,
                                             in1=bank[b][0:w, 0:wk], op0=ALU.mult, op1=ALU.add).then_inc(free[b], 1)
                for e in range(2):
                    b = n % 2 + 6 * e
                    dve.wait_ge(free[b], BASE["att"][b] + n // 2 + 1)
                dve.tensor_reduce(mx[0:w, n % 2, :, 0], S[0:w, n % 2, :, 0:wk], AX, ALU.max).then_inc(mx_done, 1)
                dve.wait_ge(mx_done, n + 1)
                for e in range(2):
                    hd = 4 * (2 * (j // 4) + e) + j % 4
                    dve.tensor_scalar(nm[0:w, n % 2, e, :], mx[0:w, n % 2, e, :], snk[0:w, hd:hd + 1], -1.0,
                                      ALU.max, ALU.mult).then_inc(nm_done, 1)

            def att_norm(n):
                j, c = UNITS[n]
                w, wk = TCS[c], sum(keys(c)[1])
                dve.wait_ge(p_done, 2 * n + 2)
                dve.wait_ge(es_done, 2 * n + 2)
                dve.tensor_tensor(den[0:w, n % 2], den[0:w, n % 2], es[0:w, n % 2], ALU.add).then_inc(den_done, 1)
                dve.wait_ge(den_done, n + 1)
                dve.reciprocal(rin[0:w, n % 2], den[0:w, n % 2]).then_inc(rin_done, 1)
                dve.wait_ge(rin_done, n + 1)
                for e in range(2):
                    dve.tensor_scalar(S[0:w, n % 2, e, 0:wk], S[0:w, n % 2, e, 0:wk], rin[0:w, n % 2, e, :], None,
                                      ALU.mult).then_inc(pn_done, 1)

            def att_low(n):
                j, c = UNITS[n]
                cols = slice(TCO[c], TCO[c] + TCS[c])
                dve.wait_ge(oh_done, n + 1)
                dve.tensor_tensor(xl[:, j, cols], bank[4 + n % 2][:, 0:TCS[c]], xh[:, j, cols].bitcast(F32),
                                  ALU.subtract).then_inc(free[4 + n % 2], 1)

            for n in range(len(UNITS) + 2):
                if n < len(UNITS):
                    att_max(n)
                if 0 <= n - 2:
                    att_low(n - 2)
                if n < len(UNITS):
                    att_norm(n)
            add_to_h("o")
            stats(4)
            apply(5, G_FFN1, h, in_g, 5)
            step = selection(1, step)
            experts(1)
            stats(5)
            apply(6, G_FIN, h, lambda dt: h[:, dt, :], None)


POOLED = 6
FIRST_AFTER = (0, 0, 1, 2, 2, 3)
SCORES_AFTER = (0, 1, 2)
SUMS_AFTER = (2, 7, 12)
ALONE_AFTER = (2, 5, 8, 11)
GATE_AFTER = (5, 6, 9, 11, 12)


def kernel(**inputs):
    import concourse.bacc as bacc
    from concourse.bass_utils import run_bass_kernel_spmd

    f = {k: np.asarray(v) for k, v in inputs.items()}

    def tiles(w):
        k, m = w.shape
        return w.reshape(k // P, P, m // P, P).transpose(2, 1, 0, 3).reshape(m // P, P, k)

    order = [4 * (2 * (j // 4) + e) + j % 4 for j in range(DT) for e in range(2)]
    wq = f["attn_w_q"][0].reshape(D, HEADS, DH)[:, order].reshape(D, D)
    wo = f["attn_w_o"][0].reshape(HEADS, DH, D)[order].reshape(D, D)
    lin = np.concatenate([tiles(w) for w in (f["gmlp_w_in"][0], f["gmlp_w_out"][0], f["peer_w_q"][0], f["w_kv"],
                                             wq, wo, f["peer_w_q"][1])])
    uv = np.empty((2, NPAIR, 4, P, D), np.float32)
    for l in range(2):
        u = f["peer_u"][l].reshape(NK, NK, DT, P)
        uv[l, :, 0:2] = u.transpose(1, 3, 2, 0).reshape(NPAIR, 2, P, D)
        v = f["peer_v"][l].reshape(NK, NPAIR, 2, 2, 512)
        uv[l, :, 2:4] = v.transpose(1, 3, 0, 2, 4).reshape(NPAIR, 2, P, D)
    x = np.concatenate([f["x_prompt"][0], f["x_sample"][0]])
    pos = np.arange(P)
    dist = np.abs(P + pos[:, None] - np.arange(2 * P)[None]).astype(np.float32)
    chunk = pos[:, None] // 64
    kchunk = np.arange(2 * P)[None] // 64
    dist[(kchunk < chunk) | (kchunk > chunk + 2)] = 1e33
    gains = np.stack([f["norm_mix"][0], f["gmlp_norm_v"][0], f["norm_ffn"][0], f["norm_kv"], f["norm_mix"][1],
                      f["norm_ffn"][1], f["norm_final"]])
    arrays = {
        "xT": x.reshape(T, DT, P).transpose(2, 1, 0),
        "ckT": f["cache_k_win"][0].reshape(P, 2, P).transpose(2, 1, 0),
        "cv": f["cache_v_win"][0].reshape(P, KVH * DH),
        "gains": gains.reshape(7, DT, P).transpose(2, 0, 1),
        "lin": lin,
        "uv": uv.reshape(2 * NPAIR * 4, P, D),
        "skT": f["peer_sub_keys"].reshape(2, HP, NK, P).transpose(0, 3, 1, 2),
        "wsT": f["gmlp_w_s"][0].transpose(2, 0, 1),
        "bs": f["gmlp_b_s"],
        "sinks": f["attn_sinks"],
        "dist": dist,
        "ident_c": np.eye(P, dtype=np.float32),
        "iota_a": np.broadcast_to(pos.astype(np.float16)[None, :, None], (P, P, TB)),
        "iota_n": np.broadcast_to(pos.astype(np.float16)[None], (P, P)),
        "iota_c": np.broadcast_to(np.arange(NC, dtype=np.float16)[None, :, None], (P, NC, TOPK)),
    }
    outs = {"yT": (P, DT, T), "kvT": (P, 4, P), "kwin": (P, 2, P), "vwin": (P, KVH * DH), "gv": (DEC, D)}
    arrays = {k: np.ascontiguousarray(a) for k, a in arrays.items()}
    nc = bacc.Bacc("TRN2", target_bir_lowering=False, num_devices=1)
    args = [nc.dram_tensor(k, a.shape, mybir.dt.from_np(a.dtype), kind="ExternalInput").ap() for k, a in arrays.items()]
    args += [nc.dram_tensor(k, s, F32, kind="ExternalOutput").ap() for k, s in outs.items()]
    parked = nc.dram_tensor("parked", (2 * AHEAD, P, 2, T), F32, kind="Internal").ap()
    program(nc, *args, parked)
    r = run_bass_kernel_spmd(nc, [arrays], core_ids=[0]).results[0]
    y = r["yT"].transpose(2, 1, 0).reshape(T, D)
    kvw = r["kvT"].transpose(2, 1, 0).reshape(P, 2, KVH, DH)
    kw = r["kwin"].transpose(2, 1, 0).reshape(1, P, KVH, DH)
    return (y[None, :SEQ], y[None, SEQ:], kvw[None, :, 0], kvw[None, :, 1], kw, r["vwin"].reshape(1, P, KVH, DH),
            r["gv"][None, None])
```

```python
from contextlib import ExitStack

import numpy as np
import concourse.bass as bass
from concourse import mybir

F32, F32R, F16, U32 = mybir.dt.float32, mybir.dt.float32r, mybir.dt.float16, mybir.dt.uint32
ALU = mybir.AluOpType
ACT = mybir.ActivationFunctionType
AX = mybir.AxisListType.X

P = 128
D, SEQ, DEC = 1024, 512, 64
T = SEQ + DEC
TH = T // 2
DT = D // P
TCS = [128, 128, 128, 128, 64]
NTC = len(TCS)
GROUPS = 8
HEADS, KVH, DH = 16, 4, 64
PH, TOPK, NK = 8, 16, 128
HP = 2 * PH
EPS = 1e-6
CHUNK = 16
NPAIR = NK // 2
STEPS = CHUNK // 2
TB = 12
NB = T // STEPS // TB
GS = 4096.0
EARLY = 2 * NTC
AHEAD = EARLY + STEPS
MAIN = NPAIR - AHEAD
NEGBIG = -3.0e38
ROWS = [TOPK // (a + 1) for a in range(TOPK // 2)]
OFFS = [sum(ROWS[:a]) for a in range(TOPK // 2 + 1)]
NC = OFFS[-1] + TOPK // 2
LIN = {"in": 16, "out": 8, "pq0": 16, "kv": 4, "q": 8, "o": 8, "pq1": 16}
G_MIX0, G_V, G_FFN0, G_KV, G_MIX1, G_FFN1, G_FIN = range(7)


def plan():
    fills, pieces, tile = [1] * 8, 0, 0
    base, kb, t0 = {}, {}, {}

    def seg(name, **use):
        base[name] = list(fills)
        for b, n in use.items():
            fills[int(b[1:])] += n

    def lin(name):
        nonlocal pieces, tile
        n = LIN[name]
        kb[name], t0[name] = pieces, tile
        pieces += n // 4
        tile += n
        return {f"b{b}": n // 2 for b in range(4)}

    def peer(l):
        nonlocal pieces
        seg(f"pq{l}", **lin(f"pq{l}"))
        seg(f"sc{l}", b4=8, b5=8, b6=8, b7=8)
        seg(f"gt{l}", b4=3, b5=2)
        seg(f"bld{l}", b6=NPAIR * NB // 2, b7=NPAIR * NB // 2)
        kb[f"peer{l}"] = pieces
        pieces += NPAIR
        seg(f"peer{l}", b0=2 * NPAIR, b1=2 * NPAIR, b2=4 * NPAIR, b3=4 * NPAIR, b4=4 * NPAIR, b5=4 * NPAIR)

    seg("n0", b6=1, b7=1)
    seg("in", **lin("in"))
    seg("n1", b6=1, b7=1)
    seg("vtr", b4=5, b5=5)
    seg("mix", b4=4, b5=4, b6=4, b7=4)
    seg("out", **lin("out"))
    seg("n2", b6=1, b7=1)
    peer(0)
    seg("n3", b6=1, b7=1)
    seg("kv", **lin("kv"))
    seg("q", **lin("q"))
    seg("vn", b6=3, b7=2)
    seg("att", **{f"b{b}": 20 for b in range(8)})
    seg("o", **lin("o"))
    seg("n4", b6=1, b7=1)
    peer(1)
    seg("n5", b6=1, b7=1)
    return base, kb, t0


def program(nc, xT, ckT, cv, gains, lin, uv, skT, wsT, bs, sinks, dist, ident_c, iota_a, iota_n, iota_c,
            yT, kvT, kwin, vwin, gv, parked):
    BASE, KB, T0 = plan()
    with ExitStack() as ctx:
        def sb(name, shape, dt):
            return ctx.enter_context(nc.sbuf_tensor(name, shape, dt))

        def sem(name):
            return ctx.enter_context(nc.semaphore(name))

        h = sb("h", [P, DT, T], F32)
        xh = sb("xh", [P, DT, T], F32R)
        xl = sb("xl", [P, DT, T], F32R)
        W = sb("W", [P, 2 * CHUNK * T], F32)
        raw = sb("raw", [P, 4, D], F32)
        wh = sb("wh", [P, 4, D], F32R)
        wl = sb("wl", [P, 4, D], F32R)
        ah = sb("ah", [P, 2, T], F32R)
        al = sb("al", [P, 2, T], F32R)
        g = sb("g", [P, 2, T], F32)
        oneA = sb("oneA", [P, 2 * P * TB // 2], F32)
        iotaA = sb("iotaA", [P, P, TB], F16)
        B = sb("B", [P, 2, TB, 2 * CHUNK], F16)
        E = sb("E", [P, 2, TB, CHUNK], F16)
        lo = sb("lo", [P, 2, TB, CHUNK], F32)
        gh = sb("gh", [P, T], F16)
        gl = sb("gl", [P, T], F16)
        i1 = sb("i1", [P, T], F16)
        i2 = sb("i2", [P, T], F16)
        ident = sb("ident", [P, P], F32)
        ones = sb("ones", [P, P], F32)
        iotaN = sb("iotaN", [P, P], F16)
        gain = sb("gain", [P, 7, DT], F32)
        bank = [ctx.enter_context(nc.psum_tensor(f"bank{b}", [P, 512], F32)) for b in range(8)]

        A = oneA[:, :].bitcast(F16).rearrange("p (s n t) -> p s n t", s=2, t=TB)
        rstd = oneA[:, 0:T]
        a2h, a2l = (v[:, 0:2, :].rearrange("p s n -> p (s n)")[:, 0:2 * T].rearrange("p (k t) -> p k t", k=2)
                    for v in (wh, wl))
        at = [0]

        def arena(*shape, dt=F32):
            n = int(np.prod(shape))
            v = W[:, at[0]:at[0] + n]
            at[0] += n
            assert at[0] <= 2 * CHUNK * T
            v = v if dt == F32 else v.bitcast(dt)
            names = " ".join("abcd"[:len(shape)])
            return v.rearrange(f"p ({names}) -> p {names}", **dict(zip("abcd", shape))) if len(shape) > 1 else v

        xf = arena(DT, T)
        at[0] = 0
        uT, vT = arena(DT, T), arena(DT, T)
        vn = arena(NTC, D)
        ws, bsb = arena(GROUPS, P), arena(GROUPS, P)
        at[0] = 0
        qT, kvs = arena(DT, T), arena(4, T)
        vnat, ck, cvs = arena(NTC, KVH * DH), arena(2, P), arena(KVH * DH)
        dst, snk = arena(2 * P), arena(HEADS)
        S = arena(SS, 2, 2 * P)
        pT = arena(2, 4, P)
        mx, nm, den, es, rin = (arena(SS, 2, 1) for _ in range(5))
        at[0] = 0
        tv = arena(NTC, HP, TOPK)
        ti = arena(NTC, HP, TOPK, dt=U32)
        tif = arena(NTC, HP, TOPK)
        icx = arena(NC * TOPK // 2).bitcast(F16).rearrange("p (c k) -> p c k", k=TOPK)
        first = at[0]
        qs = arena(4, T)
        sk = arena(HP, NK)
        scb = arena(2, NTC, NK)
        scr = arena(NTC, NK)
        at[0] = first
        prod = arena(PH, NC, TOPK)
        eq = arena(PH, NC * TOPK // 2).rearrange("p q n -> p (q n)").bitcast(F16).rearrange(
            "p (q c k) -> p q c k", q=PH, k=TOPK)
        cand, ce, cr = (arena(PH, NC) for _ in range(3))
        bv, ex, gt, es2, f1, f2 = (arena(PH, TOPK) for _ in range(6))
        bp, eu, e1, e2 = (arena(PH, TOPK, dt=U32) for _ in range(4))
        bph = arena(PH * TOPK // 2).bitcast(F16).rearrange("p (q k) -> p q k", q=PH)
        sm, rs = arena(PH), arena(PH)

        full = [sem(f"full{b}") for b in range(8)]
        free = [sem(f"free{b}") for b in range(8)]
        raw_in = [sem(f"raw_in{s}") for s in range(4)]
        hi_done = [sem(f"hi_done{s}") for s in range(4)]
        lo_done = [sem(f"lo_done{s}") for s in range(4)]
        consts_in, sample_in, attn_in, sk_in, x_in, icn_in = (sem(n) for n in (
            "consts_in", "sample_in", "attn_in", "sk_in", "x_in", "icn_in"))
        ones_done, ws_masked = sem("ones_done"), sem("ws_masked")
        sq_done, sq_used = sem("sq_done"), sem("sq_used")
        var_done, std_done, rstd_done = sem("var_done"), sem("std_done"), sem("rstd_done")
        nv_done, xh_done = sem("nv_done"), sem("xh_done")
        xl_done, xo_done = sem("xl_done"), sem("xo_done")
        vnat_done, mixu_done = sem("vnat_done"), sem("mixu_done")
        out_done = sem("out_done")
        q_ready, top_step = sem("q_ready"), sem("top_step")
        top_done, tif_done, ce_done, ce_step, cand_done, sub_done, exp_done, eq_done, pr_done, e_done, sel_done = (
            sem(n) for n in ("top_done", "tif_done", "ce_done", "ce_step", "cand_done", "sub_done", "exp_done",
                             "eq_done", "pr_done", "e_done", "sel_done"))
        gh_done, idx_done = sem("gh_done"), sem("idx_done")
        a_one, b_eq, b_one, lo_ready = sem("a_one"), sem("b_eq"), sem("b_one"), sem("lo_ready")
        prod_done, ah_done, a_done = sem("prod_done"), sem("ah_done"), sem("a_done")
        mx_done, nm_done, p_done, es_done, den_done, rin_done, pn_done, oh_done = (
            sem(n) for n in ("mx_done", "nm_done", "p_done", "es_done", "den_done", "rin_done",
                             "pn_done", "oh_done"))
        h_step = sem("h_step")
        spilled, g_in = [sem(f"spilled{t}") for t in range(2)], sem("g_in")

        HALF = [slice(0, TH), slice(TH, T)]
        TCO = [128 * c for c in range(NTC)]
        block = ctx.enter_context(nc.Block())

        UNITS = [(j, c) for j in range(DT) for c in range(NTC)]

        def keys(c):
            return (P, [P]) if c == 0 else (0, [P, P]) if c < 4 else (0, [P, DEC])

        LAST_USE = {"out": "n1", "pq0": "n2", "q": "q", "o": "vn", "pq1": "n4"}

        def first_high(eng, copy, name, s):
            eng.wait_ge(raw_in[s], 16 * KB[name] + 16)
            if name == "kv":
                eng.wait_ge(full[5], BASE["n3"][5] - (4, 4, 2, 0)[s])
            elif name in LAST_USE:
                b = 2 * (s % 2) + 1
                eng.wait_ge(full[b], BASE[LAST_USE[name]][b] - 1 + s // 2)
            copy(wh[:, s, :], raw[:, s, :]).then_inc(hi_done[s], 1)

        def low_part(eng, k, dt, done):
            eng.wait_ge(xh_done, DT * k + dt + 1)
            eng.tensor_tensor(xl[:, dt, :], xf[:, dt, :], xh[:, dt, :].bitcast(F32), ALU.subtract).then_inc(done, 1)

        def wait_low(eng, k, dt):
            if dt % 2 == 1 and k != 1:
                eng.wait_ge(xo_done, DT // 2 * (k - (k > 1)) + dt // 2 + 1)
            else:
                eng.wait_ge(xl_done, DT // 2 * (k + (k > 1)) + (dt if k == 1 else dt // 2) + 1)

        @block.sync
        def _(sp):
            def load(s, src, k):
                sp.wait_ge(lo_done[s], k + 1)
                sp.dma_start(raw[:, s, :], src).then_inc(raw_in[s], 16)

            def linear(name):
                with sp.Fori(0, LIN[name] // 4) as r:
                    for s in range(4):
                        load(s, lin[bass.ds(r * 4 + T0[name] + s, 1), :, :].rearrange("a p n -> p (a n)"),
                             r + KB[name])

            def piece(l, i, s):
                n = (i + l * NPAIR) * 4 + s
                return uv[bass.ds(n, 1), :, :].rearrange("a p n -> p (a n)")

            def experts(l):
                kb, base = KB[f"peer{l}"], BASE[f"peer{l}"]

                def u_load(k, i):
                    for s in (0, 1):
                        load(s, piece(l, i, s), k + kb)

                def v_load(i):
                    for s in (2, 3):
                        load(s, piece(l, i, s), i + kb)

                def park(k, loads):
                    n = k + AHEAD * l if isinstance(k, int) else sp.snap(k + AHEAD * l)
                    for t in range(2):
                        sp.wait_ge(free[1], k * 2 + (base[1] + t + 1))
                        sp.dma_start(parked[bass.ds(n, 1), :, t, :].rearrange("a p n -> p (a n)"),
                                     g[:, t, :]).then_inc(spilled[t], 16)
                        load(t, piece(l, loads[1], t), loads[0] + kb)

                def fetch(i):
                    n = i + (AHEAD * l - MAIN)
                    n = n if isinstance(i, int) else sp.snap(n)
                    sp.wait_ge(a_done, i * 4 + 4 * NPAIR * l)
                    sp.dma_start(g[:, :, :], parked[bass.ds(n, 1), :, :, :].rearrange(
                        "a p t n -> p (a t) n")).then_inc(g_in, 16)

                u_load(0, MAIN)
                u_load(1, MAIN + 1)
                with sp.Fori(0, AHEAD - 2) as k:
                    park(k, (k + 2, k + (MAIN + 2)))
                for k in (AHEAD - 2, AHEAD - 1):
                    park(k, (k + 2, k + 2 - AHEAD))
                with sp.Fori(0, MAIN - 2) as i:
                    v_load(i)
                    u_load(i + (AHEAD + 2), i + 2)
                v_load(MAIN - 2)
                v_load(MAIN - 1)
                for t in range(2):
                    sp.wait_ge(spilled[t], 16 * AHEAD * (l + 1))
                fetch(MAIN)
                with sp.Fori(MAIN, NPAIR - 1) as i:
                    v_load(i)
                    fetch(i + 1)
                v_load(NPAIR - 1)

            for dt in range(DT):
                sp.dma_start(h[:, dt, :], xT[:, dt, :]).then_inc(x_in, 16)
            for name in ("in", "out", "pq0"):
                linear(name)
            experts(0)
            for name in ("kv", "q", "o", "pq1"):
                linear(name)
            experts(1)
            for dt in range(DT):
                sp.wait_ge(nv_done, 6 * DT + dt + 1)
                sp.dma_start(yT[:, dt, :], h[:, dt, :]).then_inc(out_done, 16)
            sp.wait_ge(out_done, 16 * (6 + DT))

        @block.tensor
        def _(pe):
            def product(b, n, cols, terms, width=TH):
                pe.wait_ge(free[b], n)
                for t, (ahi, alo, bhi, blo) in enumerate(terms):
                    pe.matmul(cols, ahi, bhi, start=(t == 0), stop=False)
                    pe.matmul(cols, ahi, blo, start=False, stop=False)
                    mm = pe.matmul(cols, alo, bhi, start=False, stop=(t == len(terms) - 1))
                mm.then_inc(full[b], 1)

            def linear_tile(name, r, s, split):
                pe.wait_ge(lo_done[s], r + (KB[name] + 2))
                if s > 0 or split is None:
                    for half in range(2):
                        b = 2 * (s % 2) + half
                        product(b, r * 2 + (BASE[name][b] + s // 2), bank[b][:, 0:TH],
                                [(wh[:, s, P * k:P * k + P], wl[:, s, P * k:P * k + P],
                                  xh[:, k, HALF[half]], xl[:, k, HALF[half]]) for k in range(DT)])
                    return
                for b in range(2):
                    pe.wait_ge(free[b], r * 2 + BASE[name][b])
                for k in range(DT):
                    pe.wait_ge(xh_done, DT * split + k + 1)
                    wait_low(pe, split, k)
                    for half in range(2):
                        cols, whi, wlo = bank[half][:, 0:TH], wh[:, 0, P * k:P * k + P], wl[:, 0, P * k:P * k + P]
                        pe.matmul(cols, whi, xh[:, k, HALF[half]], start=(k == 0), stop=False, skip_group_check=True)
                        pe.matmul(cols, whi, xl[:, k, HALF[half]], start=False, stop=False, skip_group_check=True)
                        mm = pe.matmul(cols, wlo, xh[:, k, HALF[half]], start=False, stop=(k == DT - 1),
                                       skip_group_check=True)
                        if k == DT - 1:
                            mm.then_inc(full[half], 1)

            def linear(name, split=None, norm=None):
                def tile(r, s):
                    linear_tile(name, r, s, split)

                rounds = LIN[name] // 4
                with pe.Fori(0, rounds if norm is None else rounds - 1) as r:
                    for s in range(4):
                        tile(r, s)
                if norm is not None:
                    for s in range(4):
                        tile(rounds - 1, s)
                        for dt in (2 * s, 2 * s + 1):
                            if dt < DT - 1:
                                norm_sum(norm, dt)
                    norm_sum(norm, DT - 1)

            def norm_sums(n):
                for dt in range(DT):
                    norm_sum(n, dt)

            def norm_sum(n, dt):
                if dt == 0:
                    for half in range(2):
                        pe.wait_ge(free[6 + half], BASE[f"n{n}"][6 + half])
                pe.wait_ge(sq_done, DT * n + dt + 1)
                for half in range(2):
                    mm = pe.matmul(bank[6 + half][:, 0:TH], ones[:, :], g[:, dt % 2, HALF[half]],
                                   start=(dt == 0), stop=(dt == DT - 1), skip_group_check=True)
                    if dt == DT - 1:
                        mm.then_inc(full[6 + half], 1)
                    elif half == 1:
                        mm.then_inc(sq_used, 1)

            def selection(l):
                name, bs_ = f"pq{l}", BASE[f"sc{l}"]

                def lin_tile(r, s):
                    linear_tile(name, r, s, 2 + 3 * l)

                def scores(r, s):
                    pe.wait_ge(sk_in, 16 * (l + 1))
                    pe.wait_ge(q_ready, r * 8 + (HP * 2 * l + 2 * s + 2))
                    for b in (4 + 2 * (s % 2), 5 + 2 * (s % 2)):
                        pe.wait_ge(free[b], r * 2 + (bs_[b] + s // 2))
                    for b, tcs in ((4 + 2 * (s % 2), range(4)), (5 + 2 * (s % 2), [4])):
                        for j, c in enumerate(tcs):
                            mm = pe.matmul(bank[b][0:TCS[c], P * j:P * j + P],
                                           qs[:, s, TCO[c]:TCO[c] + TCS[c]],
                                           sk[:, bass.ds(r * 4 + s, 1), :].rearrange("p a n -> p (a n)"),
                                           start=(j == 0), stop=True, skip_group_check=True)
                        mm.then_inc(full[b], 1)

                with pe.Fori(0, HP // 4) as r:
                    lin_tile(r, 0)
                    for s in (1, 2, 3):
                        lin_tile(r, s)
                        scores(r, s - 1)
                    scores(r, 3)

            def turn(l, c):
                b = 4 + c % 2
                pe.wait_ge(sel_done, NTC * l + c + 1)
                pe.wait_ge(free[b], BASE[f"gt{l}"][b] + c // 2)
                for j, src in enumerate((gt, f1, f2)):
                    mm = pe.transpose(bank[b][:, P * j:P * j + TCS[c]],
                                      src[0:TCS[c], :, :].rearrange("p a b -> p (a b)"),
                                      ident[0:TCS[c], 0:TCS[c]])
                mm.then_inc(full[b], 1)

            def build(l, step, b):
                n = BASE[f"bld{l}"][6 + b % 2] + b // 2
                pe.wait_ge(a_one, step * NB + (NPAIR * NB * l + b + 1))
                pe.wait_ge(b_one, step * NB + (NPAIR * NB * l + b + 1))
                pe.wait_ge(free[6 + b % 2], step * (NB // 2) + n)
                for t in range(TB):
                    mm = pe.matmul(bank[6 + b % 2][:, 2 * CHUNK * t:2 * CHUNK * (t + 1)], A[:, b % 2, :, t],
                                   B[:, b % 2, t, :], start=(t == 0), stop=True, skip_group_check=True)
                mm.then_inc(full[6 + b % 2], 1)

            def expert_scores(l, k, step=None, after=()):
                for u in range(4):
                    t, half = u // 2, u % 2
                    pe.wait_ge(lo_done[t], k + (KB[f"peer{l}"] + 2))
                    product(half, k * 2 + (BASE[f"peer{l}"][half] + t), bank[half][:, 0:TH],
                            [(wh[:, t, P * d:P * d + P], wl[:, t, P * d:P * d + P],
                              xh[:, d, HALF[half]], xl[:, d, HALF[half]]) for d in range(DT)])
                    for b in [b for b, v in enumerate(after) if v == u]:
                        build(l, step, b)

            def expert_sums(l, i, step=None, after=(), b0=0, a=(ah, al), norm=None):
                pe.wait_ge(a_done, i * 4 + (4 * NPAIR * l + 4))
                for u in range(2 * DT):
                    d, half = u // 2, u % 2
                    if u in (0, DT):
                        pe.wait_ge(lo_done[2 + u // DT], i + (KB[f"peer{l}"] + 2))
                    s, o, b = 2 + d // 4, P * (d % 4), 2 + u % 4
                    product(b, i * 4 + (BASE[f"peer{l}"][b] + u // 4), bank[b][:, 0:TH],
                            [(wh[:, s, 512 * k + o:512 * k + o + P], wl[:, s, 512 * k + o:512 * k + o + P],
                              a[0][:, k, HALF[half]], a[1][:, k, HALF[half]]) for k in range(2)])
                    if u in after:
                        build(l, step, b0 + after.index(u))
                    if norm is not None and u >= 2 * NORM_LAG + 1 and u % 2 == 1:
                        norm_sum(norm, u // 2 - NORM_LAG)
                if norm is not None:
                    for dt in range(DT - NORM_LAG, DT):
                        norm_sum(norm, dt)

            def experts(l):
                for c in range(NTC):
                    expert_scores(l, 2 * c)
                    if c >= 1:
                        turn(l, c - 1)
                    expert_scores(l, 2 * c + 1)
                turn(l, NTC - 1)
                with pe.Fori(0, STEPS) as step:
                    expert_scores(l, step + EARLY, step, FIRST_AFTER)
                expert_scores(l, AHEAD)
                with pe.Fori(0, MAIN - 1) as i:
                    expert_scores(l, i + (AHEAD + 1), i + STEPS, SCORES_AFTER)
                    expert_sums(l, i, i + STEPS, SUMS_AFTER, 3)

                def alone(i, odd, building, norm=None):
                    if building:
                        for b in range(2):
                            build(l, i + STEPS, b)
                    expert_sums(l, i, i + STEPS, ALONE_AFTER if building else (), 2, (ah, al) if odd else (a2h, a2l),
                                norm)

                alone(MAIN - 1, True, True)
                with pe.Fori(0, (NPAIR - STEPS - MAIN) // 2 - 1) as j:
                    for e in range(2):
                        alone(j * 2 + (MAIN + e), e == 1, True)
                for e in range(2):
                    alone(NPAIR - STEPS - 2 + e, e == 1, True)
                with pe.Fori(0, STEPS // 2 - 1) as j:
                    for e in range(2):
                        alone(j * 2 + (NPAIR - STEPS + e), e == 1, False)
                alone(NPAIR - 2, False, False)
                alone(NPAIR - 1, True, False, 3 + 2 * l)

            for b in range(8):
                pe.nop().then_inc(full[b], 1)
            pe.wait_ge(consts_in, 16 * 4)
            pe.wait_ge(ones_done, 1)
            norm_sums(0)
            linear("in", 0, 1)
            for c in range(NTC):
                for q in range(2):
                    b = 4 + q
                    pe.wait_ge(free[b], BASE["vtr"][b] + c)
                    for k in range(4):
                        dt = 4 * q + k
                        pe.wait_ge(nv_done, DT + dt + 1)
                        mm = pe.transpose(bank[b][0:TCS[c], P * k:P * k + P], vT[:, dt, TCO[c]:TCO[c] + TCS[c]],
                                          ident[:, :])
                    mm.then_inc(full[b], 1)
            pe.wait_ge(vnat_done, 2 * NTC)
            pe.wait_ge(ws_masked, 1)
            for q in range(GROUPS):
                for b, tcs in ((4 + 2 * (q % 2), range(4)), (5 + 2 * (q % 2), [4])):
                    pe.wait_ge(free[b], BASE["mix"][b] + q // 2)
                    for j, c in enumerate(tcs):
                        mm = pe.matmul(bank[b][:, P * j:P * j + TCS[c]], vn[0:TCS[c], c, P * q:P * q + P],
                                       ws[0:TCS[c], q, 0:TCS[c]], start=(j == 0), stop=True, skip_group_check=True)
                    mm.then_inc(full[b], 1)
            linear("out", 1, 2)
            selection(0)
            experts(0)
            linear("kv", 3)
            linear("q", 4)
            pe.wait_ge(free[0], BASE["kv"][0] + 2)
            pe.wait_ge(free[1], BASE["kv"][1] + 2)
            pe.wait_ge(free[2], BASE["kv"][2] + 2)
            pe.wait_ge(free[3], BASE["kv"][3] + 2)
            for c in range(NTC):
                b = 6 + c % 2
                pe.wait_ge(free[b], BASE["vn"][b] + c // 2)
                for k in range(2):
                    mm = pe.transpose(bank[b][0:TCS[c], P * k:P * k + P], kvs[:, 2 + k, TCO[c]:TCO[c] + TCS[c]],
                                      ident[:, :])
                mm.then_inc(full[b], 1)

            def att_scores(n):
                j, c = UNITS[n]
                w, k0 = TCS[c], TCO[c]
                for e in range(2):
                    b = n % 2 + 6 * e
                    pe.wait_ge(free[b], BASE["att"][b] + n // 2)
                    r = slice(64 * e, 64 * e + 64)
                    o = 0
                    q = qT[r, j, k0:k0 + w]
                    if c == 0:
                        blocks = [kvs[r, j // 4, 0:P]]
                    elif c < 4:
                        blocks = [kvs[r, j // 4, k0 - P:k0 + P]]
                    else:
                        blocks = [ck[r, j // 4, :], kvs[r, j // 4, k0:k0 + w]]
                    for m, kk in enumerate(blocks):
                        wk = kk.shape[-1]
                        mm = pe.matmul(bank[b][0:w, o:o + wk], q, kk, start=(m == 0), stop=True,
                                       skip_group_check=True)
                        o += wk
                    mm.then_inc(full[b], 1)

            def att_turn(n):
                j, c = UNITS[n]
                w = TCS[c]
                pe.wait_ge(pn_done, 2 * n + 2)
                pe.wait_ge(free[2 + n % 2], BASE["att"][2 + n % 2] + n // 2)
                for e in range(2):
                    o = 0
                    for m, wk in enumerate(keys(c)[1]):
                        mm = pe.transpose(bank[2 + n % 2][0:wk, P * (2 * e + m):P * (2 * e + m) + w],
                                          S[0:w, n % SS, e, o:o + wk], ident[0:w, 0:w])
                        o += wk
                mm.then_inc(full[2 + n % 2], 1)

            def att_out(n):
                j, c = UNITS[n]
                w = TCS[c]
                pe.wait_ge(free[2 + n % 2], BASE["att"][2 + n % 2] + n // 2 + 1)
                pe.wait_ge(free[4 + n % 2], BASE["att"][4 + n % 2] + n // 2)
                for e in range(2):
                    kv = 2 * (j // 4) + e
                    cols = slice(DH * kv, DH * kv + DH)
                    if c == 0:
                        blocks = [vnat[:, 0, cols]]
                    elif c < 4:
                        blocks = [vnat[:, c - 1, cols], vnat[:, c, cols]]
                    else:
                        blocks = [cvs[:, cols], vnat[0:DEC, 4, cols]]
                    for m, vv in enumerate(blocks):
                        wk = keys(c)[1][m]
                        mm = pe.matmul(bank[4 + n % 2][64 * e:64 * e + 64, 0:w], vv, pT[0:wk, n % 2, 2 * e + m, 0:w],
                                       start=(m == 0), stop=(m == len(blocks) - 1), skip_group_check=True)
                mm.then_inc(full[4 + n % 2], 1)

            pe.wait_ge(attn_in, 16 * 4)
            pe.wait_ge(vnat_done, 3 * NTC)
            for b in range(4):
                pe.wait_ge(free[b], BASE["q"][b] + 4)
            for n in range(len(UNITS) + 3):
                if n < len(UNITS):
                    att_scores(n)
                if 0 <= n - 2 < len(UNITS):
                    att_turn(n - 2)
                if 0 <= n - 3:
                    att_out(n - 3)
            for b in (4, 5):
                pe.wait_ge(free[b], BASE["att"][b] + len(UNITS) // 2)
            linear("o", None, 4)
            selection(1)
            experts(1)

        @block.scalar
        def _(act):
            def square(n, src, dt):
                if dt >= 2:
                    act.wait_ge(sq_used, (DT - 1) * n + dt - 1)
                act.activation(g[:, dt % 2, :], src[:, dt, :], ACT.Square).then_inc(sq_done, 1)

            def roots(n):
                for half in range(2):
                    act.wait_ge(var_done, 2 * n + half + 1)
                    act.activation(rstd[:, HALF[half]], rstd[:, HALF[half]], ACT.Sqrt).then_inc(std_done, 1)

            def last_high(name):
                first_high(act, lambda out, in_: act.activation(out, in_, ACT.Copy), name, 3)

            def squares_of_h(n, name=None):
                for dt in range(DT):
                    if name:
                        for b in (2 * (dt % 2), 2 * (dt % 2) + 1):
                            act.wait_ge(free[b], BASE[name][b] + dt // 2 + 1)
                    square(n, h, dt)
                if name:
                    last_high(f"pq{n // 2 - 1}")
                roots(n)

            def high_parts(k, n):
                for dt in range(DT):
                    act.wait_ge(nv_done, DT * n + dt + 1)
                    act.activation(xh[:, dt, :], xf[:, dt, :], ACT.Copy).then_inc(xh_done, 1)

            def evacuate(name, fn, v_squares=False):
                def tile(r, s):
                    for half in range(2):
                        b = 2 * (s % 2) + half
                        act.wait_ge(full[b], r * 2 + (BASE[name][b] + s // 2 + 1))
                        fn(r, s, half, b).then_inc(free[b], 1)

                rounds = LIN[name] // 4
                with act.Fori(0, rounds - 1 if v_squares else rounds) as r:
                    for s in range(4):
                        tile(r, s)
                if v_squares:
                    def v_square(dt):
                        for b in (2 * (dt % 2), 2 * (dt % 2) + 1):
                            act.wait_ge(free[b], BASE[name][b] + LIN[name] // 2 - 4 + dt // 2 + 1)
                        square(1, vT, dt)

                    for s in range(4):
                        v_square(2 * s)
                        if s < 3:
                            v_square(2 * s + 1)
                        tile(rounds - 1, s)
                    v_square(DT - 1)

            def at_tile(buf, n, half):
                return buf.rearrange("p a t -> p (a t)")[:, bass.ds(n * T + TH * half, TH)]

            def high(s, k, used):
                act.wait_ge(raw_in[s], k * 16 + 16)
                act.wait_ge(full[used[0]], used[1])
                act.activation(wh[:, s, :], raw[:, s, :], ACT.Copy).then_inc(hi_done[s], 1)

            def selection(l):
                for dt in (DT - 2, DT - 1):
                    wait_low(act, 2 + 3 * l, dt)
                act.wait_ge(out_done, 16 * 3 * (l + 1))
                if l == 1:
                    act.wait_ge(h_step, 2 * 16)
                act.dma_start(sk, skT[l]).then_inc(sk_in, 16)
                act.dma_start(icx, iota_c).then_inc(icn_in, 16)

                def copy_scores(m):
                    s = m % 4
                    if m >= 2:
                        act.wait_ge(top_done, HP * l + m - 1)
                    for b, lo_, n, c0 in ((4 + 2 * (s % 2), P, 4, 0), (5 + 2 * (s % 2), DEC, 1, 4)):
                        act.wait_ge(full[b], BASE[f"sc{l}"][b] + m // 2 + 1)
                        act.activation(scb[0:lo_, m % 2, c0:c0 + n, :],
                                       bank[b][0:lo_, 0:P * n].rearrange("p (c n) -> p c n", c=n),
                                       ACT.Copy).then_inc(free[b], 1)

                name = f"pq{l}"

                def weight_high(m):
                    s, b = m % 4, 2 * (m % 2) + 1
                    act.wait_ge(raw_in[s], 16 * (KB[name] + m // 4 + 1))
                    act.wait_ge(full[b], BASE[name][b] + m // 2 - 1)
                    act.activation(wh[:, s, :], raw[:, s, :], ACT.Copy).then_inc(hi_done[s], 1)

                for m in range(HP):
                    if m >= 4:
                        act.wait_ge(full[5 + 2 * (m % 2)], BASE[f"sc{l}"][5 + 2 * (m % 2)] + m // 2 - 1)
                    for half in range(2):
                        b = 2 * (m % 2) + half
                        act.wait_ge(full[b], BASE[name][b] + m // 2 + 1)
                        act.activation(qs[:, m % 4, HALF[half]], bank[b][:, 0:TH], ACT.Copy).then_inc(q_ready, 1)
                    for half in range(2):
                        act.wait_ge(q_ready, 2 * (HP * l + m) + half + 1)
                        act.nop().then_inc(free[2 * (m % 2) + half], 1)
                    if m >= 1:
                        copy_scores(m - 1)
                    if m + 4 < HP:
                        weight_high(m + 4)
                copy_scores(HP - 1)

            def gates_high(l, c):
                b = 4 + c % 2
                act.wait_ge(full[b], BASE[f"gt{l}"][b] + c // 2 + 1)
                act.activation(gh[:, TCO[c]:TCO[c] + TCS[c]], bank[b][:, 0:TCS[c]], ACT.Copy,
                               scale=GS).then_inc(gh_done, 1)

            def gate_exp(l, c):
                act.wait_ge(sub_done, NTC * l + c + 1)
                act.activation(ex[0:TCS[c]], ex[0:TCS[c]], ACT.Exp).then_inc(exp_done, 1)

            def build(l, step, b):
                act.wait_ge(full[6 + b % 2], step * (NB // 2) + (BASE[f"bld{l}"][6 + b % 2] + b // 2 + 1))
                act.wait_ge(free[6 + b % 2], step * (NB // 2) + (BASE[f"bld{l}"][6 + b % 2] + b // 2))
                act.activation(lo[:, b % 2, :, :],
                               bank[6 + b % 2][:, 0:2 * CHUNK * TB].rearrange("p (t n) -> p t n", t=TB)[:, :, CHUNK:],
                               ACT.Copy, scale=1.0 / GS).then_inc(lo_ready, 1)

            def experts(l):
                kb, base = KB[f"peer{l}"], BASE[f"peer{l}"]

                def u_high(k, t):
                    high(t, k + kb, (1, k * 2 + (base[1] + t - 1)))

                def v_high(i):
                    for s in (2, 3):
                        high(s, i + kb, (5, i * 4 + (base[5] if s == 3 else base[5] - 2)))

                def score_step(k, parked_=False, first=False, last=False, step=None, after=()):
                    for u in range(4):
                        t, half = u // 2, u % 2
                        act.wait_ge(full[half], k * 2 + (base[half] + t + 1))
                        if parked_:
                            act.wait_ge(spilled[t], k * 16 + 16 * AHEAD * l)
                        elif not first:
                            act.wait_ge(a_done, k * 4 + (4 * NPAIR * l - 4 * (AHEAD + 1) + u + 1))
                        act.activation(g[:, t, HALF[half]], bank[half][:, 0:TH],
                                       ACT.Gelu_apprx_tanh).then_inc(free[half], 1)
                        if u % 2 == 1 and not last:
                            u_high(k + 1, t)
                        for b in [b for b, v in enumerate(after) if v == u]:
                            build(l, step, b)

                for t in range(2):
                    high(t, kb, (2 * t + 1, base[2 * t + 1]))
                for c in range(NTC):
                    score_step(2 * c, parked_=c > 0, first=c == 0)
                    gate_exp(l, c)
                    if c >= 1:
                        gates_high(l, c - 1)
                    score_step(2 * c + 1, parked_=True)
                gates_high(l, NTC - 1)
                with act.Fori(0, STEPS) as step:
                    score_step(step + EARLY, parked_=True, step=step, after=FIRST_AFTER)
                score_step(AHEAD, parked_=True)
                with act.Fori(0, MAIN - 2) as i:
                    v_high(i)
                    score_step(i + (AHEAD + 1), step=i + STEPS, after=SCORES_AFTER)
                    for b in range(3, NB):
                        build(l, i + STEPS, b)
                i = MAIN - 2
                v_high(i)
                score_step(i + AHEAD + 1, last=True, step=i + STEPS, after=SCORES_AFTER)
                for b in range(3, NB):
                    build(l, i + STEPS, b)
                with act.Fori(MAIN - 1, NPAIR - STEPS) as i:
                    v_high(i)
                    for b in range(NB):
                        build(l, i + STEPS, b)
                with act.Fori(NPAIR - STEPS, NPAIR) as i:
                    v_high(i)

            act.dma_start(ident[:, :], ident_c).then_inc(consts_in, 16)
            act.dma_start(gain[:, :, :], gains).then_inc(consts_in, 16)
            act.dma_start(iotaA[:, :, :], iota_a).then_inc(consts_in, 16)
            act.dma_start(iotaN[:, :], iota_n).then_inc(consts_in, 16)
            act.dma_start(ws, wsT).then_inc(sample_in, 16)
            act.dma_start(bsb, bs.broadcast_to([P, GROUPS, P])).then_inc(sample_in, 16)
            act.dma_start(kwin[:, :, 0:DEC], ckT[:, :, DEC:P]).then_inc(out_done, 16)
            act.dma_start(vwin[0:DEC, :], cv[DEC:P, :]).then_inc(out_done, 16)

            act.wait_ge(x_in, 16 * DT)
            squares_of_h(0)
            high_parts(0, 0)
            uv_all = W[:, 0:2 * DT * T]
            evacuate("in", lambda r, s, half, b: act.activation(
                uv_all[:, bass.ds(r * (4 * T) + (T * s + TH * half), TH)], bank[b][:, 0:TH], ACT.Gelu_apprx_tanh), True)
            roots(1)
            for c in range(NTC):
                act.wait_ge(full[4], BASE["vtr"][4] + c + 1)
                act.activation(vn[0:TCS[c], c, 0:512], bank[4][0:TCS[c], :], ACT.Copy).then_inc(free[4], 1)
            act.wait_ge(free[4], BASE["vtr"][4] + NTC)
            act.wait_ge(vnat_done, 2 * NTC)
            act.dma_start(gv, vn[0:DEC, 4, :]).then_inc(out_done, 16)
            for q in range(GROUPS):
                act.wait_ge(mixu_done, q + 1)
                act.activation(xh[:, q, :], vT[:, q, :], ACT.Copy).then_inc(xh_done, 1)
            def weights_high(name):
                with act.Fori(1, LIN[name] // 4) as r:
                    for s in range(4):
                        high(s, r + KB[name], (2 * (s % 2) + 1, r * 2 + (BASE[name][2 * (s % 2) + 1] + s // 2 - 1)))

            weights_high("out")
            squares_of_h(2, "out")
            high_parts(2, 2)
            selection(0)
            experts(0)
            def squares_of_sums(l):
                n = 3 + 2 * l
                act.wait_ge(a_done, 4 * NPAIR * (l + 1))
                for dt in range(DT):
                    for b in (2 + 2 * (dt % 2), 3 + 2 * (dt % 2)):
                        act.wait_ge(free[b], BASE[f"peer{l}"][b] + 4 * NPAIR - 3 + dt // 2)
                    square(n, h, dt)
                if l == 0:
                    last_high("kv")
                roots(n)

            squares_of_sums(0)
            act.dma_start(ck, ckT).then_inc(attn_in, 16)
            act.dma_start(cvs, cv).then_inc(attn_in, 16)
            act.dma_start(dst, dist).then_inc(attn_in, 16)
            act.dma_start(snk, sinks.broadcast_to([P, HEADS])).then_inc(attn_in, 16)
            high_parts(3, 3)
            evacuate("kv", lambda r, s, half, b: act.activation(kvs[:, s, HALF[half]], bank[b][:, 0:TH], ACT.Copy))
            high_parts(4, 4)
            evacuate("q", lambda r, s, half, b: act.activation(
                qT.rearrange("p a t -> p (a t)")[:, bass.ds(r * (4 * T) + (T * s + TH * half), TH)],
                bank[b][:, 0:TH], ACT.Copy, scale=DH ** -0.5))
            for b in range(4):
                act.wait_ge(free[b], BASE["kv"][b] + 2)
            act.dma_start(kvT, kvs[:, :, SEQ - P:SEQ]).then_inc(out_done, 16)
            act.dma_start(kwin[:, :, DEC:P], kvs[:, 0:2, SEQ:T]).then_inc(out_done, 16)
            act.wait_ge(vnat_done, 3 * NTC)
            act.dma_start(vwin[DEC:P, :], vnat[0:DEC, 4, :]).then_inc(out_done, 16)
            act.wait_ge(attn_in, 16 * 4)

            def att_exp(n):
                j, c = UNITS[n]
                w, wk = TCS[c], sum(keys(c)[1])
                for e in range(2):
                    hd = 4 * (2 * (j // 4) + e) + j % 4
                    act.wait_ge(nm_done, 2 * n + e + 1)
                    act.activation(S[0:w, n % SS, e, 0:wk], S[0:w, n % SS, e, 0:wk], ACT.Exp,
                                   bias=nm[0:w, n % SS, e, :], accum_out=den[0:w, n % SS, e, :]).then_inc(p_done, 1)
                    act.activation(es[0:w, n % SS, e, :], snk[0:w, hd:hd + 1], ACT.Exp,
                                   bias=nm[0:w, n % SS, e, :]).then_inc(es_done, 1)

            def att_copy(n):
                j, c = UNITS[n]
                w, wks = TCS[c], keys(c)[1]
                act.wait_ge(full[2 + n % 2], BASE["att"][2 + n % 2] + n // 2 + 1)
                if n >= 2:
                    act.wait_ge(full[4 + n % 2], BASE["att"][4 + n % 2] + n // 2)
                if wks == [P, P]:
                    act.activation(pT[:, n % 2, :, :], bank[2 + n % 2][:, :].rearrange("p (a q) -> p a q", a=4),
                                   ACT.Copy).then_inc(free[2 + n % 2], 1)
                    return
                src = bank[2 + n % 2][:, :].rearrange("p (e m q) -> p e m q", e=2, m=2)
                dstp = pT[:, n % 2, :, :].rearrange("p (e m) q -> p e m q", e=2)
                for m, wk in enumerate(wks):
                    a = act.activation(dstp[0:wk, :, m, 0:w], src[0:wk, :, m, 0:w], ACT.Copy)
                a.then_inc(free[2 + n % 2], 1)

            def att_high(n):
                j, c = UNITS[n]
                act.wait_ge(full[4 + n % 2], BASE["att"][4 + n % 2] + n // 2 + 1)
                act.activation(xh[:, j, TCO[c]:TCO[c] + TCS[c]], bank[4 + n % 2][:, 0:TCS[c]],
                               ACT.Copy).then_inc(oh_done, 1)

            for n in range(len(UNITS) + 3):
                if n < len(UNITS):
                    att_exp(n)
                if 0 <= n - 2 < len(UNITS):
                    att_copy(n - 2)
                if 0 <= n - 3:
                    att_high(n - 3)
            weights_high("o")
            squares_of_h(4, "o")
            high_parts(5, 5)
            selection(1)
            experts(1)
            squares_of_sums(1)

        @block.gpsimd
        def _(pool):
            def low(s, k):
                pool.wait_ge(hi_done[s], k + 1)
                pool.tensor_tensor(wl[:, s, :], raw[:, s, :], wh[:, s, :].bitcast(F32),
                                   ALU.subtract).then_inc(lo_done[s], 1)

            def weights_low(name):
                with pool.Fori(1, LIN[name] // 4) as r:
                    for s in range(4):
                        low(s, r + KB[name])

            def first_low(name):
                for s in range(4):
                    low(s, KB[name])

            def low_parts(k):
                for dt in range(0, DT, 2):
                    low_part(pool, k, dt, xl_done)

            def selection(l):
                weights_low(f"pq{l}")
                kb = KB[f"peer{l}"]
                low(0, kb)
                low(1, kb)
                pool.wait_ge(top_done, HP * (l + 1))

                def sums(c):
                    n = TCS[c]
                    f = tif[0:n, c, :, :].rearrange("p (h two) k -> p h two k", two=2)
                    t = ti[0:n, c, :, :].rearrange("p (h two) k -> p h two k", two=2)
                    pool.tensor_scalar(f[:, :, 0, :], t[:, :, 0, :], float(NK), None, ALU.mult)
                    pool.tensor_copy(f[:, :, 1, :], t[:, :, 1, :]).then_inc(tif_done, 1)
                    pool.wait_ge(tif_done, NTC * l + c + 1)
                    if c >= 1:
                        pool.wait_ge(e_done, NTC * l + c)
                    for a in range(TOPK // 2):
                        pool.tensor_tensor(ce[0:n, :, OFFS[a]:OFFS[a] + ROWS[a]],
                                           f[:, :, 0, a:a + 1].broadcast_to([n, PH, ROWS[a]]),
                                           f[:, :, 1, 0:ROWS[a]], ALU.add)
                    pool.tensor_tensor(ce[0:n, :, OFFS[-1]:NC], f[:, :, 0, TOPK // 2:TOPK],
                                       f[:, :, 1, 0:1].broadcast_to([n, PH, TOPK // 2]),
                                       ALU.add).then_inc(ce_done, 1)
                    pool.wait_ge(ce_done, NTC * l + c + 1)

                for c in range(NTC):
                    n = TCS[c]
                    sums(c)
                    for q in range(POOLED):
                        pool.wait_ge(eq_done, PH * (NTC * l + c) + q + 1)
                        pool.tensor_tensor(prod[0:n, q], eq[0:n, q], ce[0:n, q, :, None].broadcast_to([n, NC, TOPK]),
                                           ALU.mult).then_inc(pr_done, 1)
                        if q in (1, 3, 5):
                            j = 4 * c + (q - 1) // 2
                            low(j % 2, kb + 1 + j // 2)
                    if c < NTC - 1:
                        low(1, kb + 2 + 2 * c)

            def build(l, step, b, tok):
                pool.wait_ge(full[6 + b % 2], step * (NB // 2) + (BASE[f"bld{l}"][6 + b % 2] + b // 2))
                pool.wait_ge(b_eq, step * NB + (NPAIR * NB * l + b + 1))
                pool.tensor_tensor(B[:, b % 2, :, 0:CHUNK], E[:, b % 2],
                                   gh[:, bass.ds(tok, TB)][:, :, None].broadcast_to([P, TB, CHUNK]), ALU.mult)
                pool.tensor_tensor(B[:, b % 2, :, CHUNK:], E[:, b % 2],
                                   gl[:, bass.ds(tok, TB)][:, :, None].broadcast_to([P, TB, CHUNK]),
                                   ALU.mult).then_inc(b_one, 1)

            def experts(l):
                kb = KB[f"peer{l}"]

                def splits(i):
                    low(2, i + kb)
                    low(3, i + kb)

                pool.wait_ge(idx_done, NTC * (l + 1))
                with pool.Fori(0, STEPS) as step:
                    for b in range(NB):
                        build(l, step, b, step * (TB * NB) + TB * b)
                        if b == 1:
                            low(1, step + (kb + EARLY))
                        elif b == 3:
                            low(0, step + (kb + EARLY + 1))
                low(1, kb + AHEAD)
                low(0, kb + AHEAD + 1)
                low(1, kb + AHEAD + 1)
                with pool.Fori(0, MAIN - 2) as i:
                    tok = (i % STEPS) * (TB * NB)
                    for b in range(NB):
                        build(l, i + STEPS, b, tok + TB * b)
                        if b == 1:
                            splits(i)
                        elif b in (2, 3):
                            low(b - 2, i + (kb + AHEAD + 2))
                with pool.Fori(MAIN - 2, NPAIR - STEPS) as i:
                    tok = (i % STEPS) * (TB * NB)
                    for b in range(NB):
                        build(l, i + STEPS, b, tok + TB * b)
                        if b == 1:
                            splits(i)
                with pool.Fori(NPAIR - STEPS, NPAIR) as i:
                    splits(i)

            for s in range(4):
                pool.nop().then_inc(lo_done[s], 1)
            pool.memset(ones[:, :], 1.0).then_inc(ones_done, 1)
            pool.wait_ge(ones_done, 1)
            pool.wait_ge(sample_in, 16 * 2)
            pool.memset(ws[64:P, :, 0:64], 0.0).then_inc(ws_masked, 1)
            pool.wait_ge(ws_masked, 1)
            first_low("in")
            low_parts(0)
            weights_low("in")
            first_low("out")
            for q in range(GROUPS):
                pool.wait_ge(xh_done, DT + q + 1)
                pool.tensor_tensor(xl[:, q, :], vT[:, q, :], xh[:, q, :].bitcast(F32), ALU.subtract)\
                    .then_inc(xl_done, 1)
            weights_low("out")
            first_low("pq0")
            low_parts(2)
            selection(0)
            experts(0)
            first_low("kv")
            low_parts(3)
            first_low("q")
            low_parts(4)
            weights_low("q")
            first_low("o")
            for n, (j, c) in enumerate(UNITS):
                w, wk = TCS[c], sum(keys(c)[1])
                pool.wait_ge(rin_done, n + 1)
                for e in range(2):
                    pool.tensor_scalar(S[0:w, n % SS, e, 0:wk], S[0:w, n % SS, e, 0:wk], rin[0:w, n % SS, e, :], None,
                                       ALU.mult).then_inc(pn_done, 1)
            weights_low("o")
            first_low("pq1")
            low_parts(5)
            selection(1)
            experts(1)

        @block.vector
        def _(dve):
            def stats(n):
                for half in range(2):
                    b = 6 + half
                    dve.wait_ge(full[b], BASE[f"n{n}"][b] + 1)
                    dve.tensor_scalar(rstd[:, HALF[half]], bank[b][:, 0:TH], 1.0 / D, EPS,
                                      ALU.mult, ALU.add).then_inc(var_done, 1)
                for half in range(2):
                    dve.wait_ge(std_done, 2 * n + half + 1)
                    dve.reciprocal(rstd[:, HALF[half]], rstd[:, HALF[half]]).then_inc(rstd_done, 1)
                for half in range(2):
                    dve.wait_ge(rstd_done, 2 * n + half + 1)
                    dve.nop().then_inc(free[6 + half], 1)

            def apply(gi, src, out, split=None):
                for dt in range(DT):
                    dve.scalar_tensor_tensor(out=out[:, dt, :], in0=src[:, dt, :], scalar=gain[:, gi, dt:dt + 1],
                                             in1=rstd, op0=ALU.mult, op1=ALU.mult).then_inc(nv_done, 1)
                    if split is not None and dt >= 3 and dt % 2 == 1:
                        low_part(dve, split, dt - 2, xo_done)
                if split is not None:
                    low_part(dve, split, DT - 1, xo_done)

            def high(s, k, b, n):
                dve.wait_ge(raw_in[s], k * 16 + 16)
                dve.wait_ge(full[b], n)
                dve.tensor_copy(wh[:, s, :], raw[:, s, :]).then_inc(hi_done[s], 1)

            def weights_high(name):
                with dve.Fori(1, LIN[name] // 4) as r:
                    for s in range(4):
                        b = 2 * (s % 2) + 1
                        high(s, r + KB[name], b, r * 2 + (BASE[name][b] + s // 2 - 1))

            def first_highs(name, slots=range(4)):
                for s in slots:
                    first_high(dve, dve.tensor_copy, name, s)

            def add_to_h(name, following):
                hf = h[:, :, :].rearrange("p a t -> p (a t)")

                def tile(r, s):
                    for half in range(2):
                        b = 2 * (s % 2) + half
                        dve.wait_ge(full[b], r * 2 + (BASE[name][b] + s // 2 + 1))
                        cols = hf[:, bass.ds(r * (4 * T) + (T * s + TH * half), TH)]
                        dve.tensor_tensor(cols, cols, bank[b][:, 0:TH], ALU.add).then_inc(free[b], 1)

                rounds = LIN[name] // 4
                with dve.Fori(0, rounds - 1) as r:
                    for s in range(4):
                        tile(r, s)
                for s in range(4):
                    tile(rounds - 1, s)
                    if s < 3:
                        first_high(dve, dve.tensor_copy, following, s)
                for b in range(4):
                    dve.wait_ge(free[b], BASE[name][b] + LIN[name] // 2)
                dve.nop().then_inc(h_step, 16)

            def search(val, idx, src, spare, shapes, step):
                n = step
                k = len(shapes)
                for j in range(k):
                    dve.max(out=val(j)[:, 0:8], in_=src(j)).then_inc(top_step, 1)
                n += k
                for j in range(k):
                    dve.wait_ge(top_step, n - k + j + 1)
                    dve.max_index(out=idx(j)[:, 0:8], in_max=val(j)[:, 0:8], in_values=src(j)).then_inc(top_step, 1)
                    dve.match_replace(out=spare(j), in_to_replace=val(j)[:, 0:8], in_values=src(j),
                                      imm_value=NEGBIG).then_inc(top_step, 1)
                n += 2 * k
                for j in range(k):
                    dve.wait_ge(top_step, n - 2 * k + 2 * j + 2)
                    dve.max(out=val(j)[:, 8:16], in_=spare(j)).then_inc(top_step, 1)
                n += k
                for j in range(k):
                    dve.wait_ge(top_step, n - k + j + 1)
                    last = dve.max_index(out=idx(j)[:, 8:16], in_max=val(j)[:, 8:16], in_values=spare(j))
                    if j < k - 1:
                        last.then_inc(top_step, 1)
                return n + k - 1, last

            def selection(l, step):
                for m in range(HP):
                    for b in (4 + 2 * (m % 2), 5 + 2 * (m % 2)):
                        dve.wait_ge(free[b], BASE[f"sc{l}"][b] + m // 2 + 1)
                    if m >= 1:
                        dve.wait_ge(top_done, HP * l + m)
                    step, last = search(lambda c: tv[0:TCS[c], c, m, :], lambda c: ti[0:TCS[c], c, m, :],
                                        lambda c: scb[0:TCS[c], m % 2, c, :], lambda c: scr[0:TCS[c], c, :],
                                        TCS, step)
                    last.then_inc(top_done, 1)
                dve.wait_ge(icn_in, 16 * (l + 1))
                dve.wait_ge(top_done, HP * (l + 1))
                for c in range(NTC):
                    n = TCS[c]
                    v = tv[0:n, c, :, :].rearrange("p (h two) k -> p h two k", two=2)
                    for a in range(TOPK // 2):
                        dve.tensor_tensor(cand[0:n, :, OFFS[a]:OFFS[a] + ROWS[a]],
                                          v[:, :, 0, a:a + 1].broadcast_to([n, PH, ROWS[a]]),
                                          v[:, :, 1, 0:ROWS[a]], ALU.add)
                    dve.tensor_tensor(cand[0:n, :, OFFS[-1]:NC], v[:, :, 0, TOPK // 2:TOPK],
                                      v[:, :, 1, 0:1].broadcast_to([n, PH, TOPK // 2]),
                                      ALU.add).then_inc(cand_done, 1)
                    dve.wait_ge(cand_done, NTC * l + c + 1)
                    step, last = search(lambda q: bv[0:n, q, :], lambda q: bp[0:n, q, :],
                                        lambda q: cand[0:n, q, :], lambda q: cr[0:n, q, :], range(PH), step)
                    last.then_inc(top_step, 1)
                    step += 1
                    dve.wait_ge(top_step, step)
                    dve.tensor_tensor(ex[0:n], bv[0:n], bv[0:n, :, 0:1].broadcast_to([n, PH, TOPK]),
                                      ALU.subtract).then_inc(sub_done, 1)
                    dve.tensor_copy(bph[0:n], bp[0:n]).then_inc(top_step, 1)
                    step += 1
                    dve.wait_ge(top_step, step)
                    for q in range(PH):
                        dve.tensor_tensor(eq[0:n, q], icx[0:n], bph[0:n, q, None, :].broadcast_to([n, NC, TOPK]),
                                          ALU.is_equal).then_inc(eq_done, 1)
                    dve.wait_ge(ce_done, NTC * l + c + 1)
                    for q in range(POOLED, PH):
                        dve.wait_ge(eq_done, PH * (NTC * l + c) + q + 1)
                        dve.tensor_tensor(prod[0:n, q], eq[0:n, q], ce[0:n, q, :, None].broadcast_to([n, NC, TOPK]),
                                          ALU.mult).then_inc(top_step, 1)
                        step += 1
                    for q in [*range(POOLED, PH), *range(POOLED)]:
                        if q >= POOLED:
                            dve.wait_ge(top_step, step - (PH - 1 - q))
                        else:
                            dve.wait_ge(pr_done, POOLED * (NTC * l + c) + q + 1)
                        last = dve.tensor_reduce(es2[0:n, q, :], prod[0:n, q].rearrange("p c k -> p k c"), AX, ALU.add)
                    last.then_inc(e_done, 1)
                    dve.wait_ge(e_done, NTC * l + c + 1)

                    def link(ins):
                        nonlocal step
                        ins.then_inc(top_step, 1)
                        step += 1
                        dve.wait_ge(top_step, step)

                    link(dve.tensor_copy(eu[0:n], es2[0:n]))
                    link(dve.tensor_scalar(e1[0:n], eu[0:n], 7, None, ALU.logical_shift_right))
                    link(dve.tensor_scalar(e2[0:n], eu[0:n], NK - 1, None, ALU.bitwise_and))
                    if c >= 1:
                        dve.wait_ge(full[4 + (c - 1) % 2], BASE[f"gt{l}"][4 + (c - 1) % 2] + (c - 1) // 2 + 1)
                    link(dve.tensor_copy(f1[0:n], e1[0:n]))
                    link(dve.tensor_copy(f2[0:n], e2[0:n]))
                    dve.wait_ge(exp_done, NTC * l + c + 1)
                    link(dve.tensor_reduce(sm[0:n], ex[0:n], AX, ALU.add))
                    link(dve.reciprocal(rs[0:n], sm[0:n]))
                    dve.tensor_tensor(gt[0:n], ex[0:n], rs[0:n, :, None].broadcast_to([n, PH, TOPK]),
                                      ALU.mult).then_inc(sel_done, 1)
                    dve.wait_ge(sel_done, NTC * l + c + 1)
                    if c >= 1:
                        take(l, c - 1)
                take(l, NTC - 1)
                return step

            def take(l, c):
                b, n = 4 + c % 2, TCS[c]
                cols = slice(TCO[c], TCO[c] + n)
                dve.wait_ge(full[b], BASE[f"gt{l}"][b] + c // 2 + 1)
                dve.wait_ge(gh_done, NTC * l + c + 1)
                dve.tensor_copy(i1[:, cols], bank[b][:, P:P + n])
                dve.tensor_copy(i2[:, cols], bank[b][:, 2 * P:2 * P + n])
                dve.scalar_tensor_tensor(out=gl[:, cols], in0=bank[b][:, 0:n], scalar=GS, in1=gh[:, cols],
                                         op0=ALU.mult, op1=ALU.subtract).then_inc(idx_done, 1)
                dve.wait_ge(idx_done, NTC * l + c + 1)
                dve.nop().then_inc(free[b], 1)

            def one_hot(l, step, b):
                tok = (step % STEPS) * (TB * NB) + TB * b
                n2 = (step // STEPS) * CHUNK
                dve.wait_ge(full[6 + b % 2], step * (NB // 2) + (BASE[f"bld{l}"][6 + b % 2] + b // 2))
                dve.tensor_tensor(E[:, b % 2], iotaN[:, bass.ds(n2, CHUNK)][:, None, :].broadcast_to([P, TB, CHUNK]),
                                  i2[:, bass.ds(tok, TB)][:, :, None].broadcast_to([P, TB, CHUNK]),
                                  ALU.is_equal).then_inc(b_eq, 1)
                dve.tensor_tensor(A[:, b % 2], iotaA[:, :, :], i1[:, None, bass.ds(tok, TB)].broadcast_to([P, P, TB]),
                                  ALU.is_equal).then_inc(a_one, 1)

            def to_w(l, step, b, off):
                dve.wait_ge(lo_ready, step * NB + (NPAIR * NB * l + b + 1))
                src = bank[6 + b % 2][:, 0:2 * CHUNK * TB].rearrange("p (t n) -> p n t", t=TB)[:, 0:CHUNK, :]
                dst_ = W3(off)
                dve.scalar_tensor_tensor(out=dst_, in0=src, scalar=1.0 / GS,
                                         in1=lo[:, b % 2, :, :].rearrange("p t n -> p n t"),
                                         op0=ALU.mult, op1=ALU.add).then_inc(free[6 + b % 2], 1)

            def W3(off):
                return W[:, :].rearrange("p (c t) -> p c t", t=T)[:, bass.ds(off[0], CHUNK), bass.ds(off[1], TB)]

            def gate_parts(l, i, built, ahead=False, late=False):
                base = BASE[f"peer{l}"]
                tile = (i % CHUNK) * 2
                Wt = W[:, :].rearrange("p (c t) -> p c t", t=T)
                hi, lw = (a2h, a2l) if late == "even" else (ah, al)

                def products(k):
                    if k == 0:
                        for b in (6, 7):
                            dve.wait_ge(free[b], built + BASE[f"bld{l}"][b])
                        if late:
                            dve.wait_ge(g_in, i * 16 + 16 * (AHEAD * l - MAIN + 1))
                    for half in range(2):
                        if not late:
                            dve.wait_ge(free[half], i * 2 + (base[half] + 2 * AHEAD + k + 1))
                        dve.tensor_tensor(g[:, k, HALF[half]], g[:, k, HALF[half]],
                                          Wt[:, bass.ds(tile + k, 1), HALF[half]].rearrange("p a t -> p (a t)"),
                                          ALU.mult).then_inc(prod_done, 1)

                def highs():
                    dve.wait_ge(full[5], i * 4 + (base[5] - 4 if ahead else base[5]))
                    if late == "even":
                        dve.wait_ge(full[1], base[1] + 2 * NPAIR)
                    for u in range(4):
                        dve.wait_ge(prod_done, i * 4 + (4 * NPAIR * l + u + 1))
                        dve.tensor_copy(hi[:, u // 2, HALF[u % 2]], g[:, u // 2, HALF[u % 2]]).then_inc(ah_done, 1)

                def lows(k):
                    for u in (2 * k, 2 * k + 1):
                        dve.wait_ge(ah_done, i * 4 + (4 * NPAIR * l + u + 1))
                        dve.tensor_tensor(lw[:, k, HALF[u % 2]], g[:, k, HALF[u % 2]],
                                          hi[:, k, HALF[u % 2]].bitcast(F32), ALU.subtract).then_inc(a_done, 1)

                return (lambda: products(0), lambda: products(1), highs, lambda: lows(0), lambda: lows(1))

            def add_sums(l, i, u):
                b, d = 2 + u % 4, u // 2
                dve.wait_ge(full[b], i * 4 + (BASE[f"peer{l}"][b] + u // 4 + 1))
                dve.tensor_tensor(h[:, d, HALF[u % 2]], h[:, d, HALF[u % 2]], bank[b][:, 0:TH],
                                  ALU.add).then_inc(free[b], 1)

            def experts(l):
                one_hot(l, 0, 0)
                one_hot(l, 0, 1)
                with dve.Fori(0, STEPS) as step:
                    for b in range(NB):
                        to_w(l, step, b, (0, step * (TB * NB) + TB * b))
                        one_hot(l, step + (b + 2) // NB, (b + 2) % NB)

                def pair(i, early, after, own=True, ahead=None, building=True, last=False):
                    tok = (i % STEPS) * (TB * NB)
                    c0 = ((i // STEPS + 1) % 2) * CHUNK
                    built = (i + STEPS) * (NB // 2) if building else NPAIR * NB // 2

                    def batch(b):
                        to_w(l, i + STEPS, b, (c0, tok + TB * b))
                        step = i + STEPS + (b + 2) // NB
                        if not (isinstance(step, int) and step == NPAIR):
                            one_hot(l, step, (b + 2) % NB)

                    if own:
                        for part in gate_parts(l, i, built):
                            part()
                    parts = {}
                    if ahead:
                        among = ahead[1]
                        todo = gate_parts(l, i + 1, built if among else built + NB // 2 * building, True, ahead[0])
                        parts = dict(zip(GATE_AFTER if among else [None] * 5, todo))
                    if building:
                        for b in range(early):
                            batch(b)
                    for u in range(2 * DT):
                        add_sums(l, i, u)
                        if building and u in after:
                            batch(early + after.index(u))
                        if u in parts:
                            parts[u]()
                        if last and u in (5, 11):
                            first_highs("kv", (0, 1) if u == 5 else (2,))
                    if ahead and not among:
                        for part in todo:
                            part()

                with dve.Fori(0, MAIN - 1) as i:
                    pair(i, 3, SUMS_AFTER)
                kinds = ("odd", "even")
                pair(MAIN - 1, 2, ALONE_AFTER, True, ("even", False))
                for i in range(MAIN, NPAIR - 2 * STEPS):
                    pair(i, 2, ALONE_AFTER, False, (kinds[i % 2], i % STEPS != STEPS - 1))
                with dve.Fori(0, STEPS // 2 - 1) as j:
                    for e in range(2):
                        pair(j * 2 + (NPAIR - 2 * STEPS + e), 2, ALONE_AFTER, False, (kinds[e], True))
                pair(NPAIR - STEPS - 2, 2, ALONE_AFTER, False, ("odd", True))
                pair(NPAIR - STEPS - 1, 2, ALONE_AFTER, False, ("even", False))
                with dve.Fori(0, STEPS // 2 - 1) as j:
                    for e in range(2):
                        pair(j * 2 + (NPAIR - STEPS + e), 0, (), False, (kinds[e], True), building=False)
                pair(NPAIR - 2, 0, (), False, ("odd", True), building=False)
                pair(NPAIR - 1, 0, (), False, None, building=False, last=l == 0)

            step = 0
            for b in range(8):
                dve.nop().then_inc(free[b], 1)
            dve.wait_ge(consts_in, 16 * 4)
            first_highs("in")
            stats(0)
            apply(G_MIX0, h, xf, 0)
            weights_high("in")
            first_highs("out")
            stats(1)
            apply(G_V, vT, vT)
            for c in range(NTC):
                dve.wait_ge(full[5], BASE["vtr"][5] + c + 1)
                dve.tensor_copy(vn[0:TCS[c], c, 512:D], bank[5][0:TCS[c], :]).then_inc(free[5], 1)
            dve.wait_ge(free[4], BASE["vtr"][4] + NTC)
            dve.wait_ge(free[5], BASE["vtr"][5] + NTC)
            dve.nop().then_inc(vnat_done, 2 * NTC)
            dve.wait_ge(sample_in, 32)
            for q in range(GROUPS):
                ba, bb = 4 + 2 * (q % 2), 5 + 2 * (q % 2)
                dve.wait_ge(full[ba], BASE["mix"][ba] + q // 2 + 1)
                dve.tensor_tensor(vT[:, q, 0:SEQ].rearrange("p (c n) -> p c n", c=4),
                                  bank[ba][:, :].rearrange("p (c n) -> p c n", c=4),
                                  bsb[:, q, None, :].broadcast_to([P, 4, P]), ALU.add).then_inc(free[ba], 1)
                dve.wait_ge(full[bb], BASE["mix"][bb] + q // 2 + 1)
                dve.tensor_tensor(vT[:, q, SEQ:T], bank[bb][:, 0:DEC], bsb[:, q, 0:DEC], ALU.add)\
                    .then_inc(free[bb], 1)
                dve.wait_ge(free[ba], BASE["mix"][ba] + q // 2 + 1)
                dve.wait_ge(free[bb], BASE["mix"][bb] + q // 2 + 1)
                dve.tensor_tensor(vT[:, q, :], vT[:, q, :], uT[:, q, :], ALU.mult).then_inc(mixu_done, 1)
            add_to_h("out", "pq0")
            stats(2)
            apply(G_FFN0, h, xf, 2)
            step = selection(0, step)
            experts(0)
            stats(3)
            apply(G_KV, h, xf, 3)
            first_highs("q")
            for b in range(4):
                dve.wait_ge(full[b], BASE["kv"][b] + 2)
            apply(G_MIX1, h, xf, 4)
            weights_high("q")
            first_highs("o")
            for c in range(NTC):
                b = 6 + c % 2
                dve.wait_ge(full[b], BASE["vn"][b] + c // 2 + 1)
                dve.tensor_copy(vnat[0:TCS[c], c, :], bank[b][0:TCS[c], 0:KVH * DH]).then_inc(free[b], 1)
            dve.wait_ge(free[6], BASE["vn"][6] + 3)
            dve.wait_ge(free[7], BASE["vn"][7] + 2)
            dve.nop().then_inc(vnat_done, NTC)
            dve.wait_ge(attn_in, 16 * 4)

            def att_max(n):
                j, c = UNITS[n]
                w, (c0, wks) = TCS[c], keys(c)
                wk = sum(wks)
                if n >= SS:
                    b = 2 + (n - SS) % 2
                    dve.wait_ge(full[b], BASE["att"][b] + (n - SS) // 2 + 1)
                for e in range(2):
                    b = n % 2 + 6 * e
                    dve.wait_ge(full[b], BASE["att"][b] + n // 2 + 1)
                    hd = 4 * (2 * (j // 4) + e) + j % 4
                    slope = 2.0 ** (-8.0 * (hd + 1) / HEADS)
                    dve.scalar_tensor_tensor(out=S[0:w, n % SS, e, 0:wk], in0=dst[0:w, c0:c0 + wk], scalar=-slope,
                                             in1=bank[b][0:w, 0:wk], op0=ALU.mult, op1=ALU.add).then_inc(free[b], 1)
                for e in range(2):
                    b = n % 2 + 6 * e
                    dve.wait_ge(free[b], BASE["att"][b] + n // 2 + 1)
                dve.tensor_reduce(mx[0:w, n % SS, :, 0], S[0:w, n % SS, :, 0:wk], AX, ALU.max).then_inc(mx_done, 1)
                dve.wait_ge(mx_done, n + 1)
                for e in range(2):
                    hd = 4 * (2 * (j // 4) + e) + j % 4
                    dve.tensor_scalar(nm[0:w, n % SS, e, :], mx[0:w, n % SS, e, :], snk[0:w, hd:hd + 1], -1.0,
                                      ALU.max, ALU.mult).then_inc(nm_done, 1)

            def att_norm(n):
                w = TCS[UNITS[n][1]]
                dve.wait_ge(p_done, 2 * n + 2)
                dve.wait_ge(es_done, 2 * n + 2)
                dve.tensor_tensor(den[0:w, n % SS], den[0:w, n % SS], es[0:w, n % SS], ALU.add).then_inc(den_done, 1)
                dve.wait_ge(den_done, n + 1)
                dve.reciprocal(rin[0:w, n % SS], den[0:w, n % SS]).then_inc(rin_done, 1)

            def att_low(n):
                j, c = UNITS[n]
                cols = slice(TCO[c], TCO[c] + TCS[c])
                dve.wait_ge(oh_done, n + 1)
                dve.tensor_tensor(xl[:, j, cols], bank[4 + n % 2][:, 0:TCS[c]], xh[:, j, cols].bitcast(F32),
                                  ALU.subtract).then_inc(free[4 + n % 2], 1)

            for n in range(len(UNITS) + 4):
                if n < len(UNITS):
                    att_max(n)
                if 0 <= n - 1 < len(UNITS):
                    att_norm(n - 1)
                if 0 <= n - 4:
                    att_low(n - 4)
            add_to_h("o", "pq1")
            stats(4)
            apply(G_FFN1, h, xf, 5)
            step = selection(1, step)
            experts(1)
            stats(5)
            apply(G_FIN, h, h)


POOLED = 6
NORM_LAG = 2
SS = 3
FIRST_AFTER = (0, 0, 1, 2, 2, 3)
SCORES_AFTER = (0, 1, 2)
SUMS_AFTER = (2, 7, 12)
ALONE_AFTER = (2, 5, 8, 10)
GATE_AFTER = (5, 6, 9, 11, 12)


def kernel(**inputs):
    import concourse.bacc as bacc
    from concourse.bass_utils import run_bass_kernel_spmd

    f = {k: np.asarray(v) for k, v in inputs.items()}

    def tiles(w):
        k, m = w.shape
        return w.reshape(k // P, P, m // P, P).transpose(2, 1, 0, 3).reshape(m // P, P, k)

    order = [4 * (2 * (j // 4) + e) + j % 4 for j in range(DT) for e in range(2)]
    wq = f["attn_w_q"][0].reshape(D, HEADS, DH)[:, order].reshape(D, D)
    wo = f["attn_w_o"][0].reshape(HEADS, DH, D)[order].reshape(D, D)
    lin = np.concatenate([tiles(w) for w in (f["gmlp_w_in"][0], f["gmlp_w_out"][0], f["peer_w_q"][0], f["w_kv"],
                                             wq, wo, f["peer_w_q"][1])])
    uv = np.empty((2, NPAIR, 4, P, D), np.float32)
    for l in range(2):
        u = f["peer_u"][l].reshape(NK, NK, DT, P)
        uv[l, :, 0:2] = u.transpose(1, 3, 2, 0).reshape(NPAIR, 2, P, D)
        v = f["peer_v"][l].reshape(NK, NPAIR, 2, 2, 512)
        uv[l, :, 2:4] = v.transpose(1, 3, 0, 2, 4).reshape(NPAIR, 2, P, D)
    x = np.concatenate([f["x_prompt"][0], f["x_sample"][0]])
    pos = np.arange(P)
    dist = np.abs(P + pos[:, None] - np.arange(2 * P)[None]).astype(np.float32)
    chunk = pos[:, None] // 64
    kchunk = np.arange(2 * P)[None] // 64
    dist[(kchunk < chunk) | (kchunk > chunk + 2)] = 1e33
    gains = np.stack([f["norm_mix"][0], f["gmlp_norm_v"][0], f["norm_ffn"][0], f["norm_kv"], f["norm_mix"][1],
                      f["norm_ffn"][1], f["norm_final"]])
    arrays = {
        "xT": x.reshape(T, DT, P).transpose(2, 1, 0),
        "ckT": f["cache_k_win"][0].reshape(P, 2, P).transpose(2, 1, 0),
        "cv": f["cache_v_win"][0].reshape(P, KVH * DH),
        "gains": gains.reshape(7, DT, P).transpose(2, 0, 1),
        "lin": lin,
        "uv": uv.reshape(2 * NPAIR * 4, P, D),
        "skT": f["peer_sub_keys"].reshape(2, HP, NK, P).transpose(0, 3, 1, 2),
        "wsT": f["gmlp_w_s"][0].transpose(2, 0, 1),
        "bs": f["gmlp_b_s"],
        "sinks": f["attn_sinks"],
        "dist": dist,
        "ident_c": np.eye(P, dtype=np.float32),
        "iota_a": np.broadcast_to(pos.astype(np.float16)[None, :, None], (P, P, TB)),
        "iota_n": np.broadcast_to(pos.astype(np.float16)[None], (P, P)),
        "iota_c": np.broadcast_to(np.arange(NC, dtype=np.float16)[None, :, None], (P, NC, TOPK)),
    }
    outs = {"yT": (P, DT, T), "kvT": (P, 4, P), "kwin": (P, 2, P), "vwin": (P, KVH * DH), "gv": (DEC, D)}
    arrays = {k: np.ascontiguousarray(a) for k, a in arrays.items()}
    nc = bacc.Bacc("TRN2", target_bir_lowering=False, num_devices=1)
    args = [nc.dram_tensor(k, a.shape, mybir.dt.from_np(a.dtype), kind="ExternalInput").ap() for k, a in arrays.items()]
    args += [nc.dram_tensor(k, s, F32, kind="ExternalOutput").ap() for k, s in outs.items()]
    parked = nc.dram_tensor("parked", (2 * AHEAD, P, 2, T), F32, kind="Internal").ap()
    program(nc, *args, parked)
    r = run_bass_kernel_spmd(nc, [arrays], core_ids=[0]).results[0]
    y = r["yT"].transpose(2, 1, 0).reshape(T, D)
    kvw = r["kvT"].transpose(2, 1, 0).reshape(P, 2, KVH, DH)
    kw = r["kwin"].transpose(2, 1, 0).reshape(1, P, KVH, DH)
    return (y[None, :SEQ], y[None, SEQ:], kvw[None, :, 0], kvw[None, :, 1], kw, r["vwin"].reshape(1, P, KVH, DH),
            r["gv"][None, None])
```
